# Optimizing a Trainium2 kernel written in Bass

```python
import math
import jax, jax.numpy as jnp
from jax import lax
import numpy as np

D_MODEL = 1024
BATCH = 1
SEQ = 512
DEPTH = 1

GMLP_WIDTH = 512
GMLP_GROUPS = 8
GMLP_HEAD = GMLP_WIDTH // GMLP_GROUPS
CHUNK = 128
S5_WIDTH = 256
S5_GROUP_CH = 16
S5_GROUPS = S5_WIDTH // S5_GROUP_CH
S5_STATE = 64
P_TOTAL = 2 * GMLP_WIDTH + S5_WIDTH + 2 * D_MODEL
N_EXPERTS = 16
CAPACITY_FACTOR = 2
EXPERT_FF = 2048
EPS = 1e-6


def rms_norm(x, g):
    xf = x.astype(jnp.float32)
    r = lax.rsqrt(jnp.mean(xf * xf, axis=-1, keepdims=True) + EPS)
    return (xf * r * g.astype(jnp.float32)).astype(x.dtype)

def gmlp_spatial_gating(u, v, ln_g, ln_b, w_s, b_s):
    bn, seq, _ = u.shape
    vf = v.astype(jnp.float32)
    mu = jnp.mean(vf, axis=-1, keepdims=True)
    var = jnp.mean(jnp.square(vf - mu), axis=-1, keepdims=True)
    vn = (vf - mu) * lax.rsqrt(var + EPS) * ln_g.astype(jnp.float32) + ln_b.astype(jnp.float32)
    vc = vn.reshape(bn, seq // CHUNK, CHUNK, GMLP_GROUPS, GMLP_HEAD)
    z = jnp.einsum('gts,bnsgc->bntgc', w_s.astype(jnp.float32), vc) \
        + jnp.transpose(b_s.astype(jnp.float32))[:, :, None]
    return u * z.reshape(bn, seq, GMLP_WIDTH).astype(u.dtype)

def _ssm_combine(e1, e2):
    a1, b1 = e1
    a2, b2 = e2
    return a1 * a2, a2 * b1 + b2

def s5_direction(u, lam_re, lam_im, log_dt, b_re, b_im, c_re, c_im, reverse):
    f32 = jnp.float32
    lam = lax.complex(lam_re.astype(f32), lam_im.astype(f32))
    dt = jnp.exp(log_dt.astype(f32))[:, None]
    lam_bar = jnp.exp(lam * dt)
    bmat = lax.complex(b_re.astype(f32), b_im.astype(f32))
    b_bar = ((lam_bar - 1.0) / lam)[:, :, None] * bmat
    bu = jnp.einsum('gph,blgh->blgp', b_bar, u.astype(jnp.complex64))
    a = jnp.broadcast_to(lam_bar, bu.shape)
    _, states = lax.associative_scan(_ssm_combine, (a, bu), axis=1, reverse=reverse)
    cmat = lax.complex(c_re.astype(f32), c_im.astype(f32))
    return jnp.real(jnp.einsum('ghp,blgp->blgh', cmat, states))

def s5_mixer(s, lam_re, lam_im, log_dt, b_re, b_im, c_re, c_im, d_skip, w_glu, b_glu):
    bn, seq, _ = s.shape
    sf = s.astype(jnp.float32).reshape(bn, seq, S5_GROUPS, S5_GROUP_CH)
    y = (s5_direction(sf, lam_re[0], lam_im[0], log_dt[0], b_re[0], b_im[0], c_re[0], c_im[0], False)
         + s5_direction(sf, lam_re[1], lam_im[1], log_dt[1], b_re[1], b_im[1], c_re[1], c_im[1], True)
         + d_skip.astype(jnp.float32) * sf)
    y = jax.nn.gelu(y.reshape(bn, seq, S5_WIDTH), approximate=False)
    y = y * jax.nn.sigmoid(y @ w_glu.astype(jnp.float32) + b_glu.astype(jnp.float32))
    return y.astype(s.dtype)

def expert_choice_ffn(h, w_router, w_gate, w_up, w_down):
    bn, seq, dm = h.shape
    cap = CAPACITY_FACTOR * seq // N_EXPERTS
    probs = jax.nn.softmax(jnp.einsum('bld,de->ble', h, w_router).astype(jnp.float32), axis=-1)
    scores = jnp.transpose(probs, (0, 2, 1))
    gate, idx = lax.top_k(scores, cap)
    xs = jax.vmap(lambda hb, ib: hb[ib])(h, idx)
    a = jnp.einsum('becd,edf->becf', xs, w_gate)
    u = jnp.einsum('becd,edf->becf', xs, w_up)
    y = jnp.einsum('becf,efd->becd', jax.nn.silu(a) * u, w_down)
    y = (y * gate[..., None]).astype(h.dtype)
    seg = (idx + (jnp.arange(bn, dtype=jnp.int32) * seq)[:, None, None]).reshape(-1)
    out = jax.ops.segment_sum(y.reshape(-1, dm), seg, num_segments=bn * seq)
    return out.reshape(bn, seq, dm)

def first_inputs(seed: int = 0) -> dict:
    key = jax.random.key(seed)
    ks = jax.random.split(key, 32)
    f32 = jnp.float32
    nrm = lambda k, shape, scale: (jax.random.normal(k, shape, f32) * scale)
    L_ = DEPTH
    x = jax.random.normal(ks[0], (BATCH, SEQ, D_MODEL), f32)
    norm1_g = 1.0 + nrm(ks[1], (L_, D_MODEL), 0.02)
    w_in = nrm(ks[2], (L_, D_MODEL, P_TOTAL), D_MODEL ** -0.5)
    b_gate = nrm(ks[3], (L_, 2 * D_MODEL), 0.02)
    gmlp_ln_g = 1.0 + nrm(ks[4], (L_, GMLP_WIDTH), 0.02)
    gmlp_ln_b = nrm(ks[5], (L_, GMLP_WIDTH), 0.02)
    gmlp_w_s = nrm(ks[6], (L_, GMLP_GROUPS, CHUNK, CHUNK), CHUNK ** -0.5)
    gmlp_b_s = 1.0 + nrm(ks[7], (L_, GMLP_GROUPS, CHUNK), 0.1)
    dshape = (L_, 2, S5_GROUPS, S5_STATE)
    s5_lam_re = -0.5 + nrm(ks[8], dshape, 0.01)
    n_idx = jnp.arange(S5_STATE, dtype=f32)
    s5_lam_im = jnp.pi * n_idx + nrm(ks[9], dshape, 0.01)
    s5_log_dt = jax.random.uniform(ks[10], (L_, 2, S5_GROUPS), f32,
                                   minval=math.log(0.001), maxval=math.log(0.1))
    bscale = (2.0 * S5_GROUP_CH) ** -0.5
    s5_b_re = nrm(ks[11], (L_, 2, S5_GROUPS, S5_STATE, S5_GROUP_CH), bscale)
    s5_b_im = nrm(ks[12], (L_, 2, S5_GROUPS, S5_STATE, S5_GROUP_CH), bscale)
    cscale = (2.0 * S5_STATE) ** -0.5
    s5_c_re = nrm(ks[13], (L_, 2, S5_GROUPS, S5_GROUP_CH, S5_STATE), cscale)
    s5_c_im = nrm(ks[14], (L_, 2, S5_GROUPS, S5_GROUP_CH, S5_STATE), cscale)
    s5_d = nrm(ks[15], (L_, S5_GROUPS, S5_GROUP_CH), 1.0)
    s5_w_glu = nrm(ks[16], (L_, S5_WIDTH, S5_WIDTH), S5_WIDTH ** -0.5)
    s5_b_glu = nrm(ks[17], (L_, S5_WIDTH), 0.02)
    w_up_a = nrm(ks[18], (L_, GMLP_WIDTH, D_MODEL), GMLP_WIDTH ** -0.5)
    w_up_b = nrm(ks[19], (L_, S5_WIDTH, D_MODEL), S5_WIDTH ** -0.5)
    w_out = nrm(ks[20], (L_, D_MODEL, D_MODEL), D_MODEL ** -0.5)
    norm2_g = 1.0 + nrm(ks[21], (L_, D_MODEL), 0.02)
    w_router = nrm(ks[22], (L_, D_MODEL, N_EXPERTS), D_MODEL ** -0.5)
    w_gate = nrm(ks[23], (L_, N_EXPERTS, D_MODEL, EXPERT_FF), D_MODEL ** -0.5)
    w_up = nrm(ks[24], (L_, N_EXPERTS, D_MODEL, EXPERT_FF), D_MODEL ** -0.5)
    w_down = nrm(ks[25], (L_, N_EXPERTS, EXPERT_FF, D_MODEL), EXPERT_FF ** -0.5)
    final_g = 1.0 + nrm(ks[26], (D_MODEL,), 0.02)
    return {"x": x, "norm1_g": norm1_g, "w_in": w_in, "b_gate": b_gate,
            "gmlp_ln_g": gmlp_ln_g, "gmlp_ln_b": gmlp_ln_b, "gmlp_w_s": gmlp_w_s, "gmlp_b_s": gmlp_b_s,
            "s5_lam_re": s5_lam_re, "s5_lam_im": s5_lam_im, "s5_log_dt": s5_log_dt,
            "s5_b_re": s5_b_re, "s5_b_im": s5_b_im, "s5_c_re": s5_c_re, "s5_c_im": s5_c_im,
            "s5_d": s5_d, "s5_w_glu": s5_w_glu, "s5_b_glu": s5_b_glu,
            "w_up_a": w_up_a, "w_up_b": w_up_b, "w_out": w_out, "norm2_g": norm2_g,
            "w_router": w_router, "w_gate": w_gate, "w_up": w_up, "w_down": w_down,
            "final_g": final_g}

def first_block(x, norm1_g, w_in, b_gate, gmlp_ln_g, gmlp_ln_b, gmlp_w_s, gmlp_b_s,
              s5_lam_re, s5_lam_im, s5_log_dt, s5_b_re, s5_b_im, s5_c_re, s5_c_im,
              s5_d, s5_w_glu, s5_b_glu, w_up_a, w_up_b, w_out, norm2_g,
              w_router, w_gate, w_up, w_down, final_g):
    o_s5 = 2 * GMLP_WIDTH
    o_gate = o_s5 + S5_WIDTH
    for l in range(DEPTH):
        h = rms_norm(x, norm1_g[l])
        p = h @ w_in[l]
        uv = jax.nn.gelu(p[..., :o_s5], approximate=False)
        s_in = p[..., o_s5:o_gate]
        gates = jax.nn.sigmoid(p[..., o_gate:] + b_gate[l])
        g_a, g_b = gates[..., :D_MODEL], gates[..., D_MODEL:]
        br_a = gmlp_spatial_gating(uv[..., :GMLP_WIDTH], uv[..., GMLP_WIDTH:],
                                   gmlp_ln_g[l], gmlp_ln_b[l], gmlp_w_s[l], gmlp_b_s[l])
        br_b = s5_mixer(s_in, s5_lam_re[l], s5_lam_im[l], s5_log_dt[l], s5_b_re[l], s5_b_im[l],
                        s5_c_re[l], s5_c_im[l], s5_d[l], s5_w_glu[l], s5_b_glu[l])
        merged = g_a * (br_a @ w_up_a[l]) + g_b * (br_b @ w_up_b[l])
        x = x + (merged @ w_out[l]).astype(x.dtype)
        h2 = rms_norm(x, norm2_g[l])
        x = x + expert_choice_ffn(h2, w_router[l], w_gate[l], w_up[l], w_down[l]).astype(x.dtype)
    return rms_norm(x, final_g)


D_MIX = D_MODEL
D_LRU = D_MIX // 2
LRU_HEADS = 8
LRU_HEAD_DIM = D_LRU // LRU_HEADS
LRU_CONV = 4
LRU_C = 8.0
D_RET = D_MIX - D_LRU
RET_HEADS = 4
RET_HEAD_DIM = D_RET // RET_HEADS
RET_CHUNK = 128
ROPE_BASE = 10000.0
D_IN = 2 * D_LRU + 4 * D_RET
SPLITS = (D_LRU, 2 * D_LRU, 2 * D_LRU + D_RET, 2 * D_LRU + 2 * D_RET, 2 * D_LRU + 3 * D_RET)
D_FF = 3 * D_MODEL
FFN_CONV = 3
NORM_EPS = 1e-6


def rms_norm_2(x, gain):
    xf = x.astype(jnp.float32)
    y = xf * lax.rsqrt(jnp.mean(xf * xf, axis=-1, keepdims=True) + NORM_EPS)
    return (y * gain.astype(jnp.float32)).astype(x.dtype)

def causal_depthwise_conv(x, w, b):
    width, ch = w.shape
    y = lax.conv_general_dilated(
        x, w[:, None, :].astype(x.dtype), window_strides=(1,),
        padding=[(width - 1, 0)], dimension_numbers=("NWC", "WIO", "NWC"),
        feature_group_count=ch)
    return y + b.astype(x.dtype)

def _linear_recurrence_combine(left, right):
    a1, b1 = left
    a2, b2 = right
    return a1 * a2, a2 * b1 + b2

def rg_lru(x, wa, ba, wx, bx, lam):
    bsz, slen, _ = x.shape
    xf = x.astype(jnp.float32)
    xh = xf.reshape(bsz, slen, LRU_HEADS, LRU_HEAD_DIM)
    r = jax.nn.sigmoid(jnp.einsum("bshi,hij->bshj", xh, wa.astype(jnp.float32)).reshape(bsz, slen, D_LRU)
                       + ba.astype(jnp.float32))
    i = jax.nn.sigmoid(jnp.einsum("bshi,hij->bshj", xh, wx.astype(jnp.float32)).reshape(bsz, slen, D_LRU)
                       + bx.astype(jnp.float32))
    log_a = -LRU_C * r * jax.nn.softplus(-lam.astype(jnp.float32))
    a = jnp.exp(log_a)
    inp = jnp.sqrt(-jnp.expm1(2.0 * log_a)) * (i * xf)
    _, h = lax.associative_scan(_linear_recurrence_combine, (a, inp), axis=1)
    return h

def rotary(x, cos, sin):
    half = x.shape[-1] // 2
    x1, x2 = x[..., :half], x[..., half:]
    return jnp.concatenate([x1 * cos - x2 * sin, x2 * cos + x1 * sin], axis=-1)

def retention_chunkwise(q, k, v):
    bsz, slen, nh, dk = q.shape
    dv = v.shape[-1]
    c = RET_CHUNK
    n = slen // c
    log_g = jnp.log1p(-jnp.exp2(-5.0 - jnp.arange(nh, dtype=jnp.float32)))
    q = q.reshape(bsz, n, c, nh, dk)
    k = (k * (dk ** -0.5)).reshape(bsz, n, c, nh, dk)
    v = v.reshape(bsz, n, c, nh, dv)
    idx = jnp.arange(c, dtype=jnp.float32)
    diff = idx[:, None] - idx[None, :]
    decay_in = jnp.where(diff[None] >= 0, jnp.exp(jnp.maximum(diff, 0.0)[None] * log_g[:, None, None]), 0.0)
    scores = jnp.einsum("bnihd,bnjhd->bnhij", q, k) * decay_in[None, None]
    inner = jnp.einsum("bnhij,bnjhe->bnihe", scores, v)
    zeta = jnp.exp((c - 1 - idx)[None, :] * log_g[:, None])
    kv = jnp.einsum("bnjhd,bnjhe,hj->nbhde", k, v, zeta)
    g_chunk = jnp.exp(c * log_g)[None, :, None, None]

    def step(state, kv_n):
        return state * g_chunk + kv_n, state

    init = jnp.zeros((bsz, nh, dk, dv), jnp.float32)
    _, prev = lax.scan(step, init, kv)
    xi = jnp.exp((idx + 1.0)[None, :] * log_g[:, None])
    cross = jnp.einsum("bnihd,nbhde,hi->bnihe", q, prev, xi)
    return (inner + cross).reshape(bsz, slen, nh, dv)

def head_group_norm(o, gain):
    mu = jnp.mean(o, axis=-1, keepdims=True)
    var = jnp.mean(jnp.square(o - mu), axis=-1, keepdims=True)
    return (o - mu) * lax.rsqrt(var + NORM_EPS) * gain.astype(jnp.float32).reshape(RET_HEADS, RET_HEAD_DIM)

def second_inputs(seed: int = 0) -> dict:
    key = jax.random.key(seed)
    ks = jax.random.split(key, 20)
    f32 = jnp.float32

    def nrm(k, shape, fan_in):
        return jax.random.normal(k, shape, f32) * (fan_in ** -0.5)

    def gain(k, shape):
        return 1.0 + 0.05 * jax.random.normal(k, shape, f32)

    def bias(k, shape):
        return 0.02 * jax.random.normal(k, shape, f32)

    a0 = jax.random.uniform(ks[9], (DEPTH, D_LRU), f32, minval=0.9, maxval=0.999)
    return {
        "x": jax.random.normal(ks[0], (BATCH, SEQ, D_MODEL), f32),
        "norm1_gain": gain(ks[1], (DEPTH, D_MODEL)),
        "w_in": nrm(ks[2], (DEPTH, D_MODEL, D_IN), D_MODEL),
        "lru_conv_w": nrm(ks[3], (DEPTH, LRU_CONV, D_LRU), LRU_CONV),
        "lru_conv_b": bias(ks[4], (DEPTH, D_LRU)),
        "lru_gate_a_w": nrm(ks[5], (DEPTH, LRU_HEADS, LRU_HEAD_DIM, LRU_HEAD_DIM), LRU_HEAD_DIM),
        "lru_gate_a_b": bias(ks[6], (DEPTH, D_LRU)),
        "lru_gate_x_w": nrm(ks[7], (DEPTH, LRU_HEADS, LRU_HEAD_DIM, LRU_HEAD_DIM), LRU_HEAD_DIM),
        "lru_gate_x_b": bias(ks[8], (DEPTH, D_LRU)),
        "lru_lambda": jnp.log(a0) - jnp.log1p(-a0),
        "lru_norm_gain": gain(ks[10], (DEPTH, D_LRU)),
        "ret_norm_gain": gain(ks[11], (DEPTH, D_RET)),
        "w_out": nrm(ks[12], (DEPTH, D_MIX, D_MODEL), D_MIX),
        "norm2_gain": gain(ks[13], (DEPTH, D_MODEL)),
        "ffn_up_w": nrm(ks[14], (DEPTH, D_MODEL, 2 * D_FF), D_MODEL),
        "ffn_conv_w": nrm(ks[15], (DEPTH, FFN_CONV, 2 * D_FF), FFN_CONV),
        "ffn_conv_b": bias(ks[16], (DEPTH, 2 * D_FF)),
        "ffn_down_w": nrm(ks[17], (DEPTH, D_FF, D_MODEL), D_FF),
        "final_norm_gain": gain(ks[18], (D_MODEL,)),
    }

def second_block(x, norm1_gain, w_in, lru_conv_w, lru_conv_b, lru_gate_a_w, lru_gate_a_b,
              lru_gate_x_w, lru_gate_x_b, lru_lambda, lru_norm_gain, ret_norm_gain, w_out,
              norm2_gain, ffn_up_w, ffn_conv_w, ffn_conv_b, ffn_down_w, final_norm_gain):
    bsz, slen, _ = x.shape
    dt = x.dtype
    pos = jnp.arange(slen, dtype=jnp.float32)
    inv_freq = ROPE_BASE ** (-jnp.arange(0, RET_HEAD_DIM, 2, dtype=jnp.float32) / RET_HEAD_DIM)
    ang = pos[:, None] * inv_freq[None, :]
    cos = jnp.cos(ang)[:, None, :]
    sin = jnp.sin(ang)[:, None, :]

    h = x
    for l in range(DEPTH):
        u = rms_norm_2(h, norm1_gain[l])
        proj = u @ w_in[l].astype(dt)
        x_lru, g_lru, q, k, v, g_ret = jnp.split(proj, SPLITS, axis=-1)

        xc = causal_depthwise_conv(x_lru, lru_conv_w[l], lru_conv_b[l])
        hl = rg_lru(xc, lru_gate_a_w[l], lru_gate_a_b[l], lru_gate_x_w[l], lru_gate_x_b[l], lru_lambda[l])
        y_lru = rms_norm_2(hl.astype(dt) * jax.nn.gelu(g_lru), lru_norm_gain[l])

        qh = rotary(q.astype(jnp.float32).reshape(bsz, slen, RET_HEADS, RET_HEAD_DIM), cos, sin)
        kh = rotary(k.astype(jnp.float32).reshape(bsz, slen, RET_HEADS, RET_HEAD_DIM), cos, sin)
        vh = v.astype(jnp.float32).reshape(bsz, slen, RET_HEADS, RET_HEAD_DIM)
        o = head_group_norm(retention_chunkwise(qh, kh, vh), ret_norm_gain[l]).reshape(bsz, slen, D_RET)
        y_ret = o.astype(dt) * jax.nn.silu(g_ret)

        mixed = jnp.concatenate([y_lru, y_ret], axis=-1)
        h = h + mixed @ w_out[l].astype(dt)

        u = rms_norm_2(h, norm2_gain[l])
        up = causal_depthwise_conv(u @ ffn_up_w[l].astype(dt), ffn_conv_w[l], ffn_conv_b[l])
        a_branch, v_branch = jnp.split(up, 2, axis=-1)
        h = h + (jax.nn.gelu(a_branch) * v_branch) @ ffn_down_w[l].astype(dt)

    return rms_norm_2(h, final_norm_gain)


def setup_inputs(seed=0):
    out = dict(first_inputs(seed))
    for name, value in second_inputs(seed + 1).items():
        if name != "x":
            out[name + "_2"] = value
    return out


def reference(
    x, norm1_g, w_in, b_gate, gmlp_ln_g, gmlp_ln_b, gmlp_w_s, gmlp_b_s, s5_lam_re, s5_lam_im,
    s5_log_dt, s5_b_re, s5_b_im, s5_c_re, s5_c_im, s5_d, s5_w_glu, s5_b_glu, w_up_a, w_up_b,
    w_out, norm2_g, w_router, w_gate, w_up, w_down, final_g, norm1_gain_2, w_in_2, lru_conv_w_2,
    lru_conv_b_2, lru_gate_a_w_2, lru_gate_a_b_2, lru_gate_x_w_2, lru_gate_x_b_2, lru_lambda_2,
    lru_norm_gain_2, ret_norm_gain_2, w_out_2, norm2_gain_2, ffn_up_w_2, ffn_conv_w_2,
    ffn_conv_b_2, ffn_down_w_2, final_norm_gain_2,
):
    x = first_block(
        x, norm1_g, w_in, b_gate, gmlp_ln_g, gmlp_ln_b, gmlp_w_s, gmlp_b_s, s5_lam_re,
        s5_lam_im, s5_log_dt, s5_b_re, s5_b_im, s5_c_re, s5_c_im, s5_d, s5_w_glu, s5_b_glu,
        w_up_a, w_up_b, w_out, norm2_g, w_router, w_gate, w_up, w_down, final_g,
    )
    return second_block(
        x, norm1_gain_2, w_in_2, lru_conv_w_2, lru_conv_b_2, lru_gate_a_w_2, lru_gate_a_b_2,
        lru_gate_x_w_2, lru_gate_x_b_2, lru_lambda_2, lru_norm_gain_2, ret_norm_gain_2, w_out_2,
        norm2_gain_2, ffn_up_w_2, ffn_conv_w_2, ffn_conv_b_2, ffn_down_w_2, final_norm_gain_2,
    )


_drawn_inputs = setup_inputs


def setup_inputs(seed=0):
    import zlib

    import numpy as np

    out = dict(_drawn_inputs(seed))
    spreads = {}
    factors = {'b_gate': 5.367,
     'gmlp_ln_g': 4.205,
     'gmlp_ln_b': 3.741,
     's5_lam_re': 64.0,
     's5_b_re': 2.79,
     's5_b_im': 2.812,
     's5_c_im': 2.756,
     's5_b_glu': 8.0,
     'norm2_g': 2.862,
     'lru_gate_a_b_2': 29.639,
     'lru_gate_x_b_2': 8.0,
     'ret_norm_gain_2': 3.051,
     'ffn_conv_b_2': 4.537,
     'lru_norm_gain_2': 2.677}
    for name, (base, spread) in spreads.items():
        noise = np.random.default_rng([zlib.crc32(name.encode()), seed]).standard_normal(out[name].shape)
        drawn = base * np.exp(spread * noise) if base else spread * noise
        out[name] = __import__('jax').numpy.asarray(drawn.astype(out[name].dtype))
    for name, factor in factors.items():
        out[name] = (out[name] * factor).astype(out[name].dtype)
    return out
```

```python
import math
from contextlib import ExitStack

import concourse.bass as bass
import concourse.mybir as mybir
import numpy as np
from concourse.alu_op_type import AluOpType as ALU

F32 = mybir.dt.float32
F32R = mybir.dt.float32r
U32 = mybir.dt.uint32
ACT = mybir.ActivationFunctionType
AX = mybir.AxisListType

P = 128
SEQ, D = 512, 1024
NT, KD = SEQ // P, D // P
EPS = 1e-6
GW, NG = 512, 8
SW, SG, SH, SP_ = 256, 16, 16, 64
BL = 8
NB = SEQ // BL
NE, CAP, FF = 16, 64, 2048
LW, RH, HD, FF2 = 512, 4, 128, 3072
NJ = FF2 // 512
CH = 2048
NRAW, NHL = 4, 2
TWO_PI_HI = 6.28125
TWO_PI_LO = 2 * math.pi - TWO_PI_HI
MAGIC = 12582912.0
HALF_PI = math.pi / 2

PROJ = (0, 2, 3, 4, 1, 5)
ORDER = [("G", 0), ("U", 0), ("G", 1), ("U", 1), ("D", 0), ("G", 2), ("U", 2), ("D", 1), ("G", 3), ("U", 3),
         ("D", 2), ("D", 3)]
C_ID, C_II, C_ONE, C_I16, C_TOK, C_IOTA, C_MSK = 0, 128, 192, 320, 336, 340, 852
NPRM = 362
P_BG, P_GLU, P_LRE, P_LIM, P_DT, P_SD = 48, 64, 66, 82, 98, 114
P_LCV, P_LGB, P_LAM, P_LG, P_RG, P_FF = 130, 150, 158, 162, 166, 170
NSMALL, NCONST = 340, 1876


def constants():
    c = np.zeros((P, NCONST), np.float32)
    c[:, C_ID:C_ID + P] = np.eye(P)
    c[:, C_II:C_II + 64] = np.concatenate([np.eye(64), np.eye(64)])
    c[:, C_ONE:C_ONE + P] = 1.0
    c[:, C_IOTA:C_IOTA + SEQ] = np.arange(SEQ)
    c[:, C_TOK:C_TOK + NT] = np.arange(P)[:, None] + P * np.arange(NT)
    for e in range(NE):
        c[e, C_MSK + e * CAP:C_MSK + (e + 1) * CAP] = 1.0
    c[:SH, C_I16:C_I16 + SH] = np.eye(SH)
    return c


def rotary_tables():
    pos = np.arange(SEQ, dtype=np.float32)
    inv = np.float32(10000.0) ** (-np.arange(0, HD, 2, dtype=np.float32) / np.float32(HD))
    ang = (pos[:, None] * inv[None, :].astype(np.float32)).astype(np.float32)
    cos, sin = np.cos(ang).T, np.sin(ang).T
    return np.stack([np.concatenate([cos, cos]), np.concatenate([-sin, sin])], 1).astype(np.float32)


def decay_tables():
    log_g = np.log1p(-np.exp2(-5.0 - np.arange(RH)))
    diff = np.arange(SEQ)[None, :] - np.arange(P)[:, None]
    d = np.where(diff[:, None, :] >= 0, np.exp(np.maximum(diff, 0)[:, None, :] * log_g[None, :, None]), 0.0)
    return (d * HD ** -0.5).astype(np.float32)


def columns(v):
    return v.reshape(-1, P).T


def lay_out(i):
    small = np.zeros((P, NPRM), np.float32)
    gains = [i["norm1_g"], i["norm2_g"], i["final_g"], i["norm1_gain_2"], i["norm2_gain_2"], i["final_norm_gain_2"]]
    small[:, 0:P_BG] = np.concatenate([columns(g.reshape(-1)) for g in gains], 1)
    small[:, P_BG:P_BG + 16] = columns(i["b_gate"][0])
    small[:, P_GLU:P_GLU + 2] = columns(i["s5_b_glu"][0])
    for c, name in ((P_LRE, "s5_lam_re"), (P_LIM, "s5_lam_im")):
        small[:, c:c + SG] = i[name][0].transpose(0, 2, 1).reshape(P, SG)
    small[:, P_DT:P_DT + SG] = np.repeat(i["s5_log_dt"][0], SP_, axis=0)
    small[0:SH, P_SD:P_SD + SG] = i["s5_d"][0].T
    lcv = np.concatenate([i["lru_conv_w_2"][0], i["lru_conv_b_2"]])
    small[:, P_LCV:P_LGB] = lcv.reshape(5, 4, P).transpose(2, 1, 0).reshape(P, 20)
    for c, name in ((P_LGB, "lru_gate_a_b_2"), (P_LGB + 4, "lru_gate_x_b_2"), (P_LAM, "lru_lambda_2"),
                    (P_LG, "lru_norm_gain_2"), (P_RG, "ret_norm_gain_2")):
        small[:, c:c + 4] = columns(i[name][0])
    fcv = np.concatenate([i["ffn_conv_w_2"][0], i["ffn_conv_b_2"]])
    small[:, P_FF:NPRM] = fcv.reshape(4, 2, NJ, 4, P).transpose(4, 2, 1, 3, 0).reshape(P, 32 * NJ)
    s5b = np.stack([i[n][0].transpose(0, 2, 1, 3).reshape(P, SG * SH) for n in ("s5_b_re", "s5_b_im")], 1)
    s5c = np.stack([i[n][0].transpose(0, 3, 1, 2).reshape(P, SG * SH) for n in ("s5_c_re", "s5_c_im")], 1)
    bs = i["gmlp_b_s"][0].reshape(4, 2, P)
    more = {
        "small": small, "s5b": s5b, "s5c": s5c,
        "x_t": i["x"][0].T.reshape(KD, P, SEQ).transpose(1, 0, 2),
        "gmlp_ws_t": i["gmlp_w_s"][0].transpose(2, 0, 1),
        "gmlp_bs": np.repeat(bs.transpose(1, 0, 2), 64, axis=0),
        "gmlp_ln": np.concatenate([i["gmlp_ln_g"], i["gmlp_ln_b"]]),
        "consts": constants(), "rotary": rotary_tables(), "decay": decay_tables(),
    }
    return {k: np.ascontiguousarray(v) for k, v in more.items()}




class Chain:

    def __init__(self, eng, sem):
        self.eng, self.sem, self.n, self.base = eng, sem, 0, None

    def link(self, ins):
        self.n += 1
        ins.then_inc(self.sem, 1)
        self.eng.wait_ge(self.sem, self.n if self.base is None else self.base + self.n)

    def loop(self, i, n0, per):
        self.base, self.n = i * per, n0

    def after(self, n):
        self.base, self.n = None, n


def group(ap, n0, kt, nn=512):
    step = CH // nn
    return [(ap[k0 * P:min(k0 + step, kt) * P, n0:n0 + nn].rearrange("(k p) n -> p k n", p=P), min(step, kt - k0), nn)
            for k0 in range(0, kt, step)]


def weight_chunks(w):
    first = group(w["w_in"], 1024, 8, 256) + group(w["w_in"], 512, 8) + group(w["w_in"], 0, 8)
    for h in range(2):
        first += group(w["w_in"], 1280 + 512 * h, 8) + group(w["w_in"], 2304 + 512 * h, 8)
    for h in range(2):
        first += group(w["w_up_a"], 512 * h, 4) + group(w["w_up_b"], 512 * h, 2)
    for h in range(2):
        first += group(w["w_out"], 512 * h, 8)
    return first


def second_chunks(w):
    win = w["w_in_2"]
    second = []
    for c in PROJ:
        second += group(win, 512 * c, 8)
    for h in range(2):
        second += group(w["w_out_2"], 512 * h, 8)
    return dict(enumerate(second))


def ffn_up_chunk(w, col, h):
    return w["ffn_up_w_2"][512 * h:512 * h + 512, bass.ds(col, 512)] \
        .rearrange("(k p) n -> p k n", p=P), 4, 512


def ffn_down_chunk(w, row, h):
    return w["ffn_down_w_2"][bass.ds(row, 512), 512 * h:512 * h + 512].rearrange("(k p) n -> p k n", p=P), 4, 512


def build(nc, w, out):
    ctx = ExitStack()
    with ctx:
        BASE = 16512

        def at(name, shape, dt, off):
            return nc.alloc_sbuf_tensor_at(name, shape, dt, offset=BASE + int(off * 1024))

        sems, chains = {}, {}

        def sem(name):
            if name not in sems:
                sems[name] = ctx.enter_context(nc.semaphore(name))
            return sems[name]

        raw = at("raw", [P, NRAW, CH], F32, 0)
        hi = [at(f"hi{j}", [P, CH], F32R, (32, 40, 102, 110)[j]) for j in range(4)]
        lo = [at(f"lo{j}", [P, CH], F32R, (48, 56, 118, 126)[j]) for j in range(4)]
        xh = at("xh", [P, KD, SEQ], F32R, 64)
        xl = at("xl", [P, KD, SEQ], F32R, 80)
        cst = at("cst", [P, NSMALL], F32, 96)
        prm = at("prm", [P, NPRM], F32, 97.5)
        gains = prm[:, 0:P_BG].rearrange("p (n k) -> p n k", n=6)
        sm = at("sm", [P, 640], F32, 99)
        B = 102
        xt = at("xt", [P, KD, SEQ], F32, B + 89)
        xin = at("xin", [P, KD, SEQ], F32, B)
        sq = at("sq", [P, KD, SEQ], F32, B + 16)
        rb = at("rb", [P, SEQ], F32, B + 32)
        VT = at("VT", [P, 2, SG, P], F32, B)
        Zs = at("Zs", [P, 2, SG, NB], F32, B)
        T2 = at("T2", [P, 2, SG, NB], F32, B + 8)
        Sn = at("Sn", [P, 2, SG, NB], F32, B + 8)
        CO = at("CO", [P, 2, SG, P], F32, B + 16)
        INT = at("INT", [P, SG, P], F32, B + 32)
        WT = at("WT", [P, 2, SG, NB], F32, B + 40)
        RD = at("RD", [P, SG, NB], F32, B + 48)
        GQ = 4
        CL = at("CL", [P, 2, GQ, 17, SH], F32, B + 52)
        TMP = at("TMP", [P, 2, GQ * 17 * SH], F32, B + 61)
        V = at("V", [P, 2, GQ, BL, SH], F32, B + 70)
        HS = at("HS", [SH, SG, 15 * SH], F32, B + 74)
        CT = at("CT", [P, 2, SG * SH], F32, B + 91)
        BS = at("BS", [P, 2, SG, SH], F32, B + 93)
        BB = at("BB", [P, 2, SG, SH], F32, B + 95)
        BN = at("BN", [P, SG, SH], F32, B + 97)
        TY = at("TY", [P, 36, SG], F32, B + 98)
        PW = at("PW", [P, 2, SG, 9], F32, B + 100.5)
        PT = at("PT", [P, 2, SG, 17], F32, B + 101.75)
        PD = at("PD", [P, 2, SG, BL], F32, B + 104)
        stok = at("stok", [P, NT, SW], F32, B + 34)
        ytok = at("ytok", [P, NT, SW], F32, B + 52)
        sblk = at("sblk", [NB, BL * SW], F32, B + 56)
        sblkg = at("sblkg", [NB, BL * SW], F32, B + 68)
        yblk = at("yblk", [NB, BL * SW], F32, B + 56)
        U = at("U", [P, SG, NB], F32, B + 64)
        yT = at("yT", [P, 2, SEQ], F32, B + 64)
        DS = at("DS", [P, 2, SG, NB], F32, B + 68)
        vg = at("vg", [P, NT, GW], F32, B + 76)
        wsT = at("wsT", [P, NG, P], F32, B + 84)
        bsb = at("bsb", [P, 4, P], F32, B + 88)
        lnv = at("lnv", [P, 2, GW], F32, B + 90)
        uT = at("uT", [P, 4, SEQ], F32, B + 94)
        ga = [at("ga0", [P, 4, SEQ], F32, B + 76), at("ga1", [P, 4, SEQ], F32, B + 32)]
        gb = [at("gb0", [P, 4, SEQ], F32, B + 84), at("gb1", [P, 4, SEQ], F32, B + 40)]
        bah = at("bah", [P, 4, SEQ], F32R, B)
        bal = at("bal", [P, 4, SEQ], F32R, B + 8)
        bbh = at("bbh", [P, 2, SEQ], F32R, B + 16)
        bbl = at("bbl", [P, 2, SEQ], F32R, B + 20)
        ztmp = at("ztmp", [P, 2, SEQ], F32, B + 52)
        sg = at("sg", [P, 2, SEQ], F32, B + 24)
        wglu = at("wglu", [P, 2, SW], F32, B + 28)
        mrg = at("mrg", [P, 2, SEQ], F32, B + 68)

        h2t = at("h2t", [P, KD, SEQ], F32, B)
        hth = at("hth", [P, NT, D], F32R, 64)
        htl = at("htl", [P, NT, D], F32R, 80)
        wr = at("wr", [P, KD, NE], F32, B + 36)
        cst2 = at("cst2", [P, NCONST - NSMALL], F32, B + 38)
        iota = cst2[:, C_IOTA - NSMALL:C_IOTA - NSMALL + SEQ]
        msk = cst2[0:NE, C_MSK - NSMALL:C_MSK - NSMALL + NE * CAP]
        lg = at("lg", [P, NT, NE], F32, B + 44)
        st = at("st", [P, 4, NT], F32, B + 44.25)
        sc = [at(f"sc{j}", [NE, SEQ], F32, B + 45 + 2 * j) for j in range(2)]
        iv2 = at("iv2", [NE, 2, P], F32, B + 49)
        idx = at("idx", [NE, CAP], U32, B + 50)
        idm = at("idm", [NE, NE, CAP], F32, B + 51)
        idxb = at("idxb", [P, (NE + 1) * CAP], F32, B + 56)
        ivc = at("ivc", [P, 2, NE], F32, B + 60.25)
        cur = at("cur", [P, 2, 2], F32, B + 60.5)
        xe = [at(f"xe{j}", [P, KD, P], F32R, B + (61, 40)[j]) for j in range(2)]
        As = [at(f"As{j}", [P, 512], F32, B + 65 + 2 * j) for j in range(2)]
        Us = [at(f"Us{j}", [P, 512], F32, B + 69 + 2 * j) for j in range(2)]
        sil = at("sil", [P, 256], F32, B + 73)
        hf = at("hf", [P, 256], F32, B + 74)
        hs = [at(f"hs{j}", [P, 4, P], F32R, B + 75 + 2 * j) for j in range(2)]
        s1 = at("s1", [P, NT, CAP], F32R, B + 79)
        yg = at("yg", [P, D], F32, B + 80)
        t1 = [at(f"t1{j}", [P, SEQ], F32R, B + 84 + 2 * j) for j in range(2)]
        yh = [at(f"yh{j}", [P, D], F32R, B + 44 + 4 * j) for j in range(2)]
        yl = [at(f"yl{j}", [P, D], F32R, B + (32, 52)[j]) for j in range(2)]

        qr = at("qr", [P, RH, SEQ], F32, B)
        kr = at("kr", [P, RH, SEQ], F32, B + 8)
        v2 = at("v2", [P, NT, RH * HD], F32, B + 16)
        gl = at("gl", [P, 4, SEQ], F32, B + 24)
        rot = at("rot", [P, 2, SEQ], F32, B + 32)
        bd = at("bd", [P, 2, 4, P], F32, B + 36)
        dec = at("dec", [P, RH, SEQ], F32, B + 40)
        sq2 = at("sq2", [P, KD, SEQ], F32, B + 48)
        h3 = at("h3", [P, KD, SEQ], F32, B + 64)
        rb2 = at("rb2", [P, SEQ], F32, B + 80)
        xc = at("xc", [P, 4, SEQ], F32, B + 48)
        rA = at("rA", [P, 4, SEQ], F32, B + 56)
        iA = at("iA", [P, 4, SEQ], F32, B + 64)
        aA = at("aA", [P, 4, SEQ], F32, B + 72)
        qs = at("qs", [P, RH, SEQ], F32, B + 80)
        sw = [at(f"sw{j}", [P, 1280], F32, B + (80, 32)[j]) for j in range(2)]
        gr = at("gr", [P, 4, SEQ], F32, 72)
        ca = at("ca", [P, 4, SEQ], F32, B)
        cv = at("cv", [P, 4, SEQ], F32, B + 8)
        aH = [at(f"aH{j}", [P, 4, SEQ], F32R, B + 16 + 8 * j) for j in range(2)]
        aL = [at(f"aL{j}", [P, 4, SEQ], F32R, B + 32 + 8 * j) for j in range(2)]
        fp = at("fp", [P, 2, 2, 4, 4], F32, B + 88)

        def lz(j):
            return sm[:, 200 + 4 * j:204 + 4 * j]

        ps = ctx.enter_context(nc.psum_tensor("ps", [P, 8, 512], F32))
        PP, QQ = 0, 4

        ident = cst[:, C_ID:C_ID + P]
        eps = sm[:, 0:1]
        ones = cst[:, C_ONE:C_ONE + P]

        first = weight_chunks(w)
        NFIRST = len(first)
        NEXP = NFIRST + 24 * NE
        NWIDE = NEXP + 4
        second = second_chunks(w)
        NFFN = NEXP + len(second)
        chunks = dict(enumerate(first)) | {NEXP + j: c for j, c in second.items()}
        wg = w["w_gate"].rearrange("e d f -> (e d) f")
        wu = w["w_up"].rearrange("e d f -> (e d) f")
        wd = w["w_down"].rearrange("e f d -> (e f) d")

        def expert_chunk(i, u, j):
            kind, c = ORDER[j // 2]
            h = j % 2
            if kind == "D":
                row = i * (2 * FF) + (u * FF + 512 * c + 256 * h)
                return wd[bass.ds(row, 256), :].rearrange("(k p) n -> p k n", p=P), 2, D
            row = i * (2 * D) + (u * D + 512 * h)
            return (wg if kind == "G" else wu)[bass.ds(row, 512), 512 * c:512 * c + 512] \
                .rearrange("(k p) n -> p k n", p=P), 4, 512

        def num(n, i, per=1, add=0):
            return n // per + add if i is None else i[0] * (i[1] // per) + (n // per + add)

        def ring(n):
            if n < NFIRST:
                return n % 2, n - 1
            if n < NWIDE:
                return n % 4, NFIRST if n < NFIRST + 4 else n - 3
            if n < NWIDE + 2:
                return n % 2, 1 + max(m for m in range(NEXP, NWIDE) if m % 4 == n % 2)
            return n % 2, n - 1

        def load_chunk(sp, n, i=None, chunk=None):
            src, nk, nn = chunk or chunks[n]
            if n >= NRAW:
                sp.wait_ge(sem("lo_done"), num(n, i, 1, 1 - NRAW))
            sp.dma_start(raw[:, n % NRAW, 0:nk * nn].rearrange("p (k n) -> p k n", k=nk), src) \
                .then_inc(sem(f"raw_in{n % NRAW}"), 16)

        def make_hi(act, n, i=None, size=CH):
            if i is None and n in chunks:
                size = chunks[n][1] * chunks[n][2]
            slot, used = ring(n)
            turn = 16 * (n // NRAW + 1)
            act.wait_ge(sem(f"raw_in{n % NRAW}"), turn if i is None else i[0] * (16 * i[1] // NRAW) + turn)
            if used > 0:
                act.wait_ge(sem("pe_used"), num(used, i))
            act.activation(hi[slot][:, 0:size], raw[:, n % NRAW, 0:size], ACT.Copy).then_inc(sem("hi_done"), 1)

        def make_lo(dve, n, i=None, size=CH):
            if i is None and n in chunks:
                size = chunks[n][1] * chunks[n][2]
            slot, used = ring(n)
            dve.wait_ge(sem("hi_done"), num(n, i, 1, 1))
            if used > 0:
                dve.wait_ge(sem("pe_used"), num(used, i))
            dve.tensor_tensor(lo[slot][:, 0:size], raw[:, n % NRAW, 0:size], hi[slot][:, 0:size].bitcast(F32),
                              ALU.subtract).then_inc(sem("lo_done"), 1)

        def dense(pe, bank, n0, ktiles, ah, al, token_major, nn=512, i=None, between=None):
            step = CH // nn
            n = n0
            for k0 in range(0, ktiles, step):
                nk = min(step, ktiles - k0)
                last = k0 + nk == ktiles
                if between and k0:
                    pe.wait_ge(*between)
                slot = ring(n)[0]
                pe.wait_ge(sem("hi_done"), num(n, i, 1, 1))
                for part in range(2):
                    if part == 1:
                        pe.wait_ge(sem("lo_done"), num(n, i, 1, 1))
                    wt = (hi, lo)[part][slot]
                    for m in range(4):
                        for kk in range(nk):
                            k = k0 + kk
                            if token_major:
                                wv = wt[:, kk * nn:(kk + 1) * nn]
                                ops = [(t[:, k, m * P:(m + 1) * P], wv) for t in ((ah, al), (ah,))[part]]
                            else:
                                wv = wt[:, kk * nn + m * P:kk * nn + (m + 1) * P]
                                ops = [(wv, t[:, k, :]) for t in ((ah, al), (ah,))[part]]
                            for q, (l, r) in enumerate(ops):
                                mm = pe.matmul(ps[:, bank + m, 0:nn if token_major else SEQ], l, r,
                                               start=(k == 0 and part == 0 and q == 0),
                                               stop=(last and part == 1 and kk == nk - 1))
                mm.then_inc(sem("pe_used"), 1)
                n += 1

        def squares(i):
            return (sq, rb) if i < 2 else (sq2, rb2)

        def norm_squares(act, i, x, after=None):
            for k in range(KD):
                if after is not None:
                    act.wait_ge(sem("nrm_x"), KD * after + k + 1)
                act.activation(squares(i)[0][:, k, :], x[:, k, :], ACT.Square).then_inc(sem("nrm_sq"), 1)

        def norm_sums(pe, i, bank):
            for k in range(KD):
                pe.wait_ge(sem("nrm_sq"), KD * i + k + 1)
                mm = pe.matmul(ps[:, bank, :], ones, squares(i)[0][:, k, :], start=(k == 0), stop=(k == KD - 1))
            mm.then_inc(sem("nrm_ps"), 1)

        def norm_root(act, i, bank):
            act.wait_ge(sem("nrm_ps"), i + 1)
            act.wait_ge(sem("eps_done"), 1)
            act.activation(squares(i)[1][:], ps[:, bank, :], ACT.Sqrt, scale=1.0 / D, bias=eps) \
                .then_inc(sem("nrm_rms"), 1)

        def norm_scale(dve, ch, i, x, dst=None):
            r = squares(i)[1]
            dve.wait_ge(sem("nrm_rms"), i + 1)
            ch.link(dve.reciprocal(r[:], r[:]))
            for k in range(KD):
                dve.scalar_tensor_tensor((dst or x)[:, k, :], x[:, k, :], gains[:, i, k:k + 1], r[:],
                                         ALU.mult, ALU.mult).then_inc(sem("nrm_x"), 1)

        def norm_round(act, i, x):
            for k in range(KD):
                act.wait_ge(sem("nrm_x"), KD * i + k + 1)
                act.activation(xh[:, k, :], x[:, k, :], ACT.Copy).then_inc(sem("xh_done"), 1)

        def norm_rest(dve, i, x):
            split = KD * {0: 0, 3: 1, 4: 2}[i]
            for k in range(KD):
                dve.wait_ge(sem("xh_done"), split + k + 1)
                dve.tensor_tensor(xl[:, k, :], x[:, k, :], xh[:, k, :].bitcast(F32), ALU.subtract) \
                    .then_inc(sem("xl_done"), 1)

        block = ctx.enter_context(nc.Block())

        GA, UA, TA, YA, XA, SA = 0, 1, 2, 3, 5, (5, 6, 7)

        def gather(pe):
            for k in range(KD):
                for half, h in enumerate((hth, htl)):
                    o = ps[:, XA + k // 4, (k % 4) * P + CAP * half:(k % 4) * P + CAP * (half + 1)]
                    for t in range(NT):
                        mm = pe.matmul(o, h[:, t, k * P:(k + 1) * P], s1[:, t, :], start=(t == 0), stop=(t == NT - 1))
            mm.then_inc(sem("gx_ps"), 1)

        def scatter(pe, i):
            def at_turn(per, add):
                return (NE // 2) * per + add if i is None else i * per + add

            pe.wait_ge(sem("yl_done"), at_turn(2, 1))
            pe.wait_ge(sem("t1_done"), at_turn(2, 1))
            pe.wait_ge(sem("xe_done"), at_turn(2, 1))
            for m in range(KD):
                if m >= 3:
                    pe.wait_ge(sem("sc_taken"), at_turn(KD, m - 1))
                for e in range(2):
                    for part, yy in enumerate((yh, yl)):
                        mm = pe.matmul(ps[:, SA[m % 3], :], yy[e][:, m * P:(m + 1) * P], t1[e][:],
                                       start=(e == 0 and part == 0), stop=(e == 1 and part == 1))
                mm.then_inc(sem("sc_ps"), 1)

        def experts_pe(pe):
            pe.wait_ge(sem("x1_done"), KD)
            norm_sums(pe, 1, 0)
            pe.wait_ge(sem("nrm_x"), 2 * KD)
            pe.wait_ge(sem("wr_in"), 32)
            for t in range(NT):
                for k in range(KD):
                    mm = pe.matmul(ps[:, 7, t * NE:(t + 1) * NE], h2t[:, k, t * P:(t + 1) * P], wr[:, k, :],
                                   start=(k == 0), stop=(k == KD - 1))
            mm.then_inc(sem("lg_ps"), 1)
            for t in range(NT):
                if t == 3:
                    pe.wait_ge(sem("htl_done"), 1)
                for k in range(KD):
                    b = 2 * (t % 3) + k // 4
                    mm = pe.transpose(ps[:, b, (k % 4) * P:(k % 4 + 1) * P], h2t[:, k, t * P:(t + 1) * P], ident)
                mm.then_inc(sem("hT_ps"), 1)
            pe.wait_ge(sem("pr_done"), 1)
            for t in range(NT):
                mm = pe.transpose(ps[0:NE, 6, t * P:(t + 1) * P], lg[:, t, :], ident)
            mm.then_inc(sem("pT_ps"), 1)
            pe.wait_ge(sem("iv_done"), 1)
            for r in range(2):
                mm = pe.transpose(ps[:, 7, r * NE:(r + 1) * NE], iv2[:, r, :], ident[0:NE, 0:NE])
            mm.then_inc(sem("ivT_ps"), 1)
            pe.wait_ge(sem("htl_done"), NT)
            pe.wait_ge(sem("idm_done"), 1)
            for h in range(2):
                mm = pe.matmul(ps[:, h, :], ones[0:NE, :], idm[:, 8 * h:8 * h + 8, :].rearrange("e a b -> e (a b)"),
                               start=True, stop=True)
            mm.then_inc(sem("idb_ps"), 1)
            pe.wait_ge(sem("s1_done"), 1)
            gather(pe)
            pe.sem_inc(sem("sc_ps"), 1)
            with pe.Fori(0, NE // 2) as i:
                for u in range(2):
                    n0 = NFIRST + 24 * u

                    def passes(j, mms):
                        n = n0 + j
                        for part in range(2):
                            pe.wait_ge(sem(("hi_done", "lo_done")[part]), num(n, (i, 48), 1, 1))
                            mm = mms((hi, lo)[part][ring(n)[0]], part)
                        mm.then_inc(sem("pe_used"), 1)
                        return mm

                    def up(j, bank, h):
                        def mms(wt, part):
                            for kk in range(4):
                                k = 4 * h + kk
                                mm = pe.matmul(ps[:, bank, :], xe[u][:, k, :], wt[:, kk * 512:(kk + 1) * 512],
                                               start=(k == 0 and part == 0), stop=(k == 7 and part == 1))
                            return mm
                        passes(j, mms)

                    def down(j, c, h):
                        def mms(wt, part):
                            for kk in range(2):
                                f = 2 * h + kk
                                for nn in range(2):
                                    mm = pe.matmul(ps[:, YA + nn, :], hs[c % 2][:, f, :],
                                                   wt[:, kk * D + nn * 512:kk * D + (nn + 1) * 512],
                                                   start=(c == 0 and f == 0 and part == 0),
                                                   stop=(c == 3 and f == 3 and part == 1))
                            return mm
                        passes(j, mms)

                    def sum_turn(c):
                        pe.wait_ge(sem("a_taken"), i * 8 + (4 * u + c + 2))
                        pe.wait_ge(sem("u_taken"), i * 8 + (4 * u + c + 2))
                        pe.wait_ge(sem("t_taken"), i * 8 + (4 * u + c + 1))
                        for r, src in enumerate((As, Us)):
                            for f in range(4):
                                mm = pe.matmul(ps[:, TA, 256 * r + CAP * f:256 * r + CAP * (f + 1)],
                                               src[c % 2][:, f * P:(f + 1) * P], cst[:, C_II:C_II + CAP],
                                               start=True, stop=True)
                        mm.then_inc(sem("t_ps"), 1)

                    for q, (kind, c) in enumerate(ORDER):
                        if kind == "G":
                            if c == 0:
                                pe.wait_ge(sem("xe_done"), i * 2 + (u + 1))
                            pe.wait_ge(sem("a_taken"), i * 8 + (4 * u + c + 1))
                            for h in range(2):
                                up(2 * q + h, GA, h)
                            if c:
                                sum_turn(c - 1)
                        elif kind == "U":
                            pe.wait_ge(sem("u_taken"), i * 8 + (4 * u + c + 1))
                            for h in range(2):
                                up(2 * q + h, UA, h)
                            if u == 0 and c == 0:
                                scatter(pe, i)
                        else:
                            if c == 0:
                                pe.wait_ge(sem("y_taken"), i * 2 + (u + 1))
                            pe.wait_ge(sem("hid_done"), i * 8 + (4 * u + c + 1))
                            down(2 * q, c, 0)
                            if c == 1:
                                pe.wait_ge(sem("s1_done"), i * 2 + (u + 2))
                                pe.wait_ge(sem("sc_taken"), i * 8 + 9)
                                pe.wait_ge(sem("xe_done"), i * 2 + (u + 1))
                                gather(pe)
                            if c == 2:
                                sum_turn(3)
                            down(2 * q + 1, c, 1)
            scatter(pe, None)

        def experts_act(act, a):
            for name in ("a_taken", "u_taken", "hsh_done", "y_taken"):
                act.sem_inc(sem(name), 1)
            act.wait_ge(sem("x1_done"), KD)
            norm_squares(act, 1, xt)
            norm_root(act, 1, 0)
            for t in range(NT):
                act.wait_ge(sem("hT_ps"), t + 1)
                b = 2 * (t % 3)
                a(hth[:, t, :], ps[:, b:b + 2, :].rearrange("p a b -> p (a b)"), ACT.Copy).then_inc(sem("hth_done"), 1)
            act.wait_ge(sem("lgm_done"), 1)
            a(lg[:], lg[:], ACT.Exp).then_inc(sem("lge_done"), 1)
            make_hi(act, NFIRST)
            act.wait_ge(sem("htl_done"), NT)
            for j in range(1, 4):
                make_hi(act, NFIRST + j)
            act.wait_ge(sem("gx_ps"), 1)
            a(xe[0][:].rearrange("p k c -> p (k c)"), ps[:, XA:XA + 2, :].rearrange("p a b -> p (a b)"), ACT.Copy) \
                .then_inc(sem("xe_done"), 1)
            with act.Fori(0, NE // 2) as i:
                for u in range(2):
                    n0 = NFIRST + 24 * u

                    def W(name, per, v):
                        act.wait_ge(sem(name), i * per + v)

                    def evac(c, r):
                        name = "au"[r]
                        act.wait_ge(sem("pe_used"), num(n0 + 2 * ORDER.index(("GU"[r], c)), (i, 48), 1, 2))
                        a((As, Us)[r][c % 2][:], ps[:, (GA, UA)[r], :], ACT.Copy).then_inc(sem(name + "_taken"), 1)

                    def silu(c):
                        W("t_ps", 8, 4 * u + c + 1)
                        W("t_taken", 8, 4 * u + c + 1)
                        a(sil[:], ps[:, TA, 0:256], ACT.Silu).then_inc(sem("sil_done"), 1)

                    def hs_hi(c):
                        W("t_taken", 8, 4 * u + c + 2)
                        a(hs[c % 2][:, :, 0:CAP], hf[:].rearrange("p (f s) -> p f s", f=4), ACT.Copy) \
                            .then_inc(sem("hsh_done"), 1)

                    for j in range(4, 28):
                        make_hi(act, n0 + j, (i, 48))
                        if j == 4:
                            evac(0, 0)
                        if j == 5:
                            evac(0, 1)
                        for c, ja, ju in ((1, 7, 9), (2, 13, 15), (3, 19, 21)):
                            if j == ja:
                                evac(c, 0)
                                silu(c - 1)
                                hs_hi(c - 1)
                            if j == ju:
                                evac(c, 1)
                        if j == 18:
                            W("gx_ps", 2, u + 2)
                            a(xe[1 - u][:].rearrange("p k c -> p (k c)"), ps[:, XA:XA + 2, :].rearrange("p a b -> p (a b)"),
                              ACT.Copy).then_inc(sem("xe_done"), 1)
                        if j == 22:
                            silu(3)
                            hs_hi(3)
                        if j == 26:
                            act.wait_ge(sem("pe_used"), num(n0, (i, 48), 1, 24))
                            W("cur_done", 2, u + 1)
                            W("yl_done", 2, u + 1)
                            a(yg[:], ps[:, YA:YA + 2, :].rearrange("p a b -> p (a b)"), ACT.Copy, scale=cur[:, u, 1:2]) \
                                .then_inc(sem("y_taken"), 1)
                            W("y_taken", 2, u + 2)
                            W("sc_ps", KD, KD + 1)
                            a(yh[u][:], yg[:], ACT.Copy).then_inc(sem("yh_done"), 1)

        def experts_dve(dve, L):
            tt, ts = dve.tensor_tensor, dve.tensor_scalar
            for name in ("t_taken", "sc_taken"):
                dve.sem_inc(sem(name), 1)
            dve.wait_ge(sem("x1_done"), KD)
            norm_scale(dve, chains["dve"], 1, xt, h2t)
            for t in range(NT):
                dve.wait_ge(sem("hth_done"), t + 1)
                b = 2 * (t % 3)
                tt(htl[:, t, :], ps[:, b:b + 2, :].rearrange("p a b -> p (a b)"), hth[:, t, :].bitcast(F32),
                   ALU.subtract).then_inc(sem("htl_done"), 1)
                if t == 0:
                    dve.wait_ge(sem("lg_ps"), 1)
                    L(dve.tensor_copy(lg[:].rearrange("p t e -> p (t e)"), ps[:, 7, 0:NT * NE]))
                    L(dve.tensor_reduce(st[:, 0, :], lg[:], AX.X, ALU.max))
                    tt(lg[:], lg[:], st[:, 0, :].unsqueeze(2).to_broadcast([P, NT, NE]), ALU.subtract) \
                        .then_inc(sem("lgm_done"), 1)
            make_lo(dve, NFIRST)
            dve.wait_ge(sem("lge_done"), 1)
            L(dve.tensor_reduce(st[:, 1, :], lg[:], AX.X, ALU.add))
            L(dve.reciprocal(st[:, 2, :], st[:, 1, :]))
            tt(lg[:], lg[:], st[:, 2, :].unsqueeze(2).to_broadcast([P, NT, NE]), ALU.mult).then_inc(sem("pr_done"), 1)
            dve.wait_ge(sem("pT_ps"), 1)
            L(dve.tensor_copy(sc[0][:], ps[0:NE, 6, :]))
            for r in range(CAP // 8):
                src, dst = sc[r % 2], sc[(r + 1) % 2]
                o = slice(8 * r, 8 * r + 8)
                L(dve.max(iv2[:, 1, o], src[:]))
                dve.max_index(idx[:, o], iv2[:, 1, o], src[:])
                L(dve.match_replace(dst[:], iv2[:, 1, o], src[:], -1.0))
            dve.tensor_copy(iv2[:, 1, CAP:P], iv2[:, 1, 0:CAP])
            dve.tensor_copy(iv2[:, 0, 0:CAP], idx[:])
            L(dve.tensor_copy(iv2[:, 0, CAP:P], idx[:]))
            dve.sem_inc(sem("iv_done"), 1)
            dve.wait_ge(sem("wr_in"), 32)
            tt(idm[:], msk.rearrange("e (a b) -> e a b", a=NE),
               iv2[:, 0, 0:CAP].unsqueeze(1).to_broadcast([NE, NE, CAP]), ALU.mult).then_inc(sem("idm_done"), 1)
            dve.memset(idxb[:, NE * CAP:], 0.0)
            for j in range(2):
                dve.memset(hs[j][:].bitcast(F32), 0.0)
            dve.wait_ge(sem("ivT_ps"), 1)
            dve.tensor_copy(ivc[:].rearrange("p r e -> p (r e)"), ps[:, 7, 0:2 * NE])
            dve.wait_ge(sem("idb_ps"), 1)
            L(dve.tensor_copy(idxb[:, 0:NE * CAP], ps[:, 0:2, :].rearrange("p a b -> p (a b)")))

            def one_hot(src):
                for t in range(NT):
                    last = ts(s1[:, t, :], src, cst[:, C_TOK + t:C_TOK + t + 1], None, ALU.is_equal)
                last.then_inc(sem("s1_done"), 1)

            one_hot(idxb[:, 0:CAP])
            for e in range(2):
                for z in (yh[e], yl[e], t1[e]):
                    last = dve.memset(z[:].bitcast(F32), 0.0)
            last.then_inc(sem("zeroed"), 1)
            dve.wait_ge(sem("zeroed"), 1)
            for name in ("yl_done", "t1_done"):
                dve.sem_inc(sem(name), 1)
            for j in range(1, 4):
                make_lo(dve, NFIRST + j)
            with dve.Fori(0, NE // 2) as i:
                for u in range(2):
                    n0 = NFIRST + 24 * u

                    def W(name, per, v):
                        dve.wait_ge(sem(name), i * per + v)

                    def product(c):
                        W("sil_done", 8, 4 * u + c + 1)
                        W("hsh_done", 8, 4 * u + c + 1)
                        tt(hf[:], sil[:], ps[:, TA, 256:512], ALU.mult).then_inc(sem("t_taken"), 1)
                        W("hsh_done", 8, 4 * u + c + 2)
                        tt(hs[c % 2][:, :, CAP:P], hf[:].rearrange("p (f s) -> p f s", f=4),
                           hs[c % 2][:, :, 0:CAP].bitcast(F32), ALU.subtract).then_inc(sem("hid_done"), 1)

                    for j in range(4, 28):
                        make_lo(dve, n0 + j, (i, 48))
                        for c, ja in ((1, 7), (2, 13), (3, 19), (4, 22)):
                            if j == ja:
                                product(c - 1)
                        if j == 5 and u == 0:
                            for m in range(KD):
                                W("sc_ps", KD, m + 2)
                                tt(xt[:, m, :], xt[:, m, :], ps[:, SA[m % 3], :], ALU.add).then_inc(sem("sc_taken"), 1)
                        if j == 7:
                            W("sc_ps", KD, KD + 1)
                            dve.tensor_copy(cur[:, u, :], ivc[:, :, bass.ds(i * 2 + u, 1)].rearrange("p r e -> p (r e)")) \
                                .then_inc(sem("cur_done"), 1)
                            W("cur_done", 2, u + 1)
                            ts(t1[u][:], iota, cur[:, u, 0:1], None, ALU.is_equal).then_inc(sem("t1_done"), 1)
                            W("gx_ps", 2, u + 1)
                            one_hot(idxb[:, bass.ds(i * (2 * CAP) + (u + 1) * CAP, CAP)])
                        if j == 26:
                            W("yh_done", 2, u + 1)
                            tt(yl[u][:], yg[:], yh[u][:].bitcast(F32), ALU.subtract).then_inc(sem("yl_done"), 1)
            for m in range(KD):
                dve.wait_ge(sem("sc_ps"), KD * (NE // 2) + m + 2)
                tt(xt[:, m, :], xt[:, m, :], ps[:, SA[m % 3], :], ALU.add).then_inc(sem("sc_taken"), 1)


        N2, SCS = NEXP, 1 + KD * (NE // 2 + 1)

        def second_pe(pe):
            pe.wait_ge(sem("sc_taken"), SCS)
            norm_sums(pe, 2, PP)
            norm_sums(pe, 3, PP + 1)
            pe.wait_ge(sem("xl_done"), 2 * KD)
            dense(pe, PP, N2, KD, xh, xl, False)
            dense(pe, QQ, N2 + 2, KD, xh, xl, False)
            pe.wait_ge(sem("xc_done"), 1)
            pe.wait_ge(sem("bd_in"), 64)
            for r in range(2):
                if r:
                    pe.wait_ge(sem("swap_done"), 2)
                    pe.wait_ge(sem("cos_done"), 1)
                for m in range(4):
                    mm = pe.matmul(ps[:, (PP, QQ)[r] + m, :], bd[:, r, m, :], xc[:, m, :], start=True, stop=True)
                    mm.then_inc(sem("lg2_ps"), 1)
            pe.wait_ge(sem("lgate_done"), 4)
            dense(pe, PP, N2 + 4, KD, xh, xl, False)
            pe.wait_ge(sem("lgate_done"), 8)
            dense(pe, QQ, N2 + 6, KD, xh, xl, True)
            pe.wait_ge(sem("swap_done"), 4)
            pe.wait_ge(sem("cos_done"), 2)
            dense(pe, PP, N2 + 8, KD, xh, xl, False)
            pe.wait_ge(sem("v2_done"), 1)
            dense(pe, QQ, N2 + 10, KD, xh, xl, False)

            def scores(h):
                if h >= 2:
                    pe.wait_ge(sem("dec_done"), h - 1)
                for J in range(4):
                    mm = pe.matmul(score(h, J), kr[:, h, J * P:(J + 1) * P], qr[:, h, J * P:], start=True, stop=True)
                mm.then_inc(sem("sco_ps"), 1)

            def values(h):
                pe.wait_ge(sem("dec_done"), h + 1)
                if h >= 2:
                    pe.wait_ge(sem("o_done"), h - 1)
                for J in range(4):
                    mm = pe.matmul(ps[:, (3, 7)[h % 2], J * P:], v2[:, J, h * P:(h + 1) * P], weights(h, J),
                                   start=(J == 0), stop=(J == 3))
                mm.then_inc(sem("av_ps"), 1)

            pe.wait_ge(sem("gl_done"), 1)
            pe.wait_ge(sem("lsq_done"), 4)
            for m in range(4):
                mm = pe.matmul(ps[:, 3, :], ones, xc[:, m, :], start=(m == 0), stop=(m == 3))
            mm.then_inc(sem("lsum_ps"), 1)
            pe.wait_ge(sem("rot_done"), 2)
            scores(0)
            pe.wait_ge(sem("gr_done"), 1)
            scores(1)
            pe.wait_ge(sem("lrms_done"), 1)
            values(0)
            scores(2)
            values(1)
            scores(3)
            values(2)
            values(3)
            for h in range(RH):
                pe.wait_ge(sem("o_done"), h + 1)
                pe.matmul(ps[:, BM[h], :], ones, qr[:, h, :], start=True, stop=True).then_inc(sem("mean_ps"), 1)
            for h in range(RH):
                pe.wait_ge(sem("csq_done"), h + 1)
                pe.matmul(ps[:, BM[h], :], ones, kr[:, h, :], start=True, stop=True).then_inc(sem("hvar_ps"), 1)
            pe.wait_ge(sem("dec_done"), RH)
            pe.wait_ge(sem("mix_lo"), 4)
            dense(pe, QQ, N2 + 12, KD, xh, xl, False, between=(sem("mix_lo"), KD))
            pe.wait_ge(sem("hstd_done"), RH)
            dense(pe, PP, N2 + 14, KD, xh, xl, False)
            pe.wait_ge(sem("x3_done"), KD)
            norm_sums(pe, 4, PP)
            pe.wait_ge(sem("xl_done"), 3 * KD)

            def part(n, i, j, down=True):
                if down:
                    pe.wait_ge(sem("dn_taken"), lin(j, i, 2, -1))
                dense(pe, PP, n, KD, xh, xl, False, i=i)
                if down:
                    pe.wait_ge(sem("dn_taken"), lin(j, i, 2, 0))
                dense(pe, QQ, n + 2, KD, xh, xl, False, i=i)
                if down:
                    way_down(n + 4, i, j, j[0] - 1)

            def way_down(n, i, j, jd):
                pe.wait_ge(sem("act_lo"), lin(j, i, 1, jd - j[0] + 1))
                pe.wait_ge(sem("fa_done"), lin(j, i, 1, 1))
                dense(pe, PP, n, 4, aH[jd % 2], aL[jd % 2], False, i=i)
                pe.wait_ge(sem("fv_done"), lin(j, i, 1, 1))
                dense(pe, QQ, n + 1, 4, aH[jd % 2], aL[jd % 2], False, i=i)

            part(NFFN, None, (0, 0), down=False)
            with pe.Fori(0, NJ // 2 - 1) as i:
                for u in range(2):
                    part(NFFN + 4 + 6 * u, (i, 12), (1 + u, 2))
            part(NFFN + 28, None, (NJ - 1, 0))
            pe.wait_ge(sem("dn_taken"), 2 * NJ)
            way_down(NFFN + 34, None, (NJ - 1, 0), NJ - 1)
            pe.wait_ge(sem("dn_taken"), 2 * NJ + 2)
            norm_sums(pe, 5, PP)

        def lin(j, i, mult, add):
            return mult * j[0] + add if i is None else i[0] * (mult * j[1]) + (mult * j[0] + add)

        BM = (0, 1, 2, 3)

        def score(h, J):
            b = (0, 4)[h % 2]
            return (ps[:, b, :], ps[:, b + 1, 0:384], ps[:, b + 2, 0:256], ps[:, b + 1, 384:512])[J]

        def weights(h, J):
            o = (0, 512, 896, 1152, 1280)
            return sw[h % 2][:, o[J]:o[J + 1]]

        def second_act(act, a):
            act.wait_ge(sem("sc_taken"), SCS)
            norm_squares(act, 2, xt)
            norm_root(act, 2, PP)
            norm_squares(act, 3, xt, after=2)
            norm_root(act, 3, PP + 1)
            norm_round(act, 3, h3)
            act.wait_ge(sem("laz_done"), 1)
            a(lz(1), lz(0), ACT.Exp, scale=-1.0).then_inc(sem("lze_done"), 1)
            act.wait_ge(sem("lzu_done"), 1)
            a(lz(3), lz(2), ACT.Ln).then_inc(sem("lzl_done"), 1)
            act.wait_ge(sem("pe_used"), N2 + 2)
            for m in range(4):
                c = P_LCV + 5 * m
                last = a(xc[:, m, :], ps[:, PP + m, :], ACT.Identity, scale=prm[:, c + 3:c + 4], bias=prm[:, c + 4:c + 5])
            last.then_inc(sem("tap_done"), 1)
            make_hi(act, N2 + 4)

            def swap(bank):
                for o, f in ((0, 64), (64, 0)):
                    a(qs[o:o + 64], ps[f:f + 64, bank:bank + 4, :], ACT.Copy).then_inc(sem("swap_done"), 1)

            def round_mixed(tiles):
                for m in tiles:
                    act.wait_ge(sem("mix_done"), m + 1)
                    a(xh[:, m, :], mixed(m), ACT.Copy).then_inc(sem("mix_hi"), 1)

            act.wait_ge(sem("pe_used"), N2 + 4)
            swap(QQ)
            make_hi(act, N2 + 5)
            for r, dst in enumerate((rA, iA)):
                for m in range(4):
                    act.wait_ge(sem("lg2_ps"), 4 * r + m + 1)
                    c = P_LGB + 4 * r + m
                    a(dst[:, m, :], ps[:, (PP, QQ)[r] + m, :], ACT.Sigmoid, bias=prm[:, c:c + 1]) \
                        .then_inc(sem("lgate_done"), 1)
            make_hi(act, N2 + 6)
            act.wait_ge(sem("lam_done"), 1)
            act.wait_ge(sem("lgate_done"), 4)
            for m in range(4):
                last = a(aA[:, m, :], rA[:, m, :], ACT.Exp, scale=lz(5)[:, m:m + 1])
            last.then_inc(sem("la_done"), 1)
            act.wait_ge(sem("la_done"), 1)
            for m in range(4):
                last = a(rA[:, m, :], rA[:, m, :], ACT.Tanh, scale=lz(4)[:, m:m + 1])
            last.then_inc(sem("tanh_done"), 1)
            act.wait_ge(sem("pe_used"), N2 + 6)
            act.wait_ge(sem("rot_done"), 1)
            swap(PP)
            make_hi(act, N2 + 7)
            act.wait_ge(sem("rad_done"), 1)
            a(rA[:], rA[:], ACT.Sqrt).then_inc(sem("root_done"), 1)
            make_hi(act, N2 + 8)
            act.wait_ge(sem("pe_used"), N2 + 8)
            a(v2[:], ps[:, QQ:QQ + 4, :], ACT.Copy).then_inc(sem("v2_done"), 1)
            make_hi(act, N2 + 9)
            make_hi(act, N2 + 10)
            act.wait_ge(sem("pe_used"), N2 + 10)
            a(gl[:], ps[:, PP:PP + 4, :], ACT.Gelu_apprx_tanh).then_inc(sem("gl_done"), 1)
            make_hi(act, N2 + 11)
            make_hi(act, N2 + 12)
            act.wait_ge(sem("hy_done"), 1)
            for m in range(4):
                a(xc[:, m, :], rA[:, m, :], ACT.Square).then_inc(sem("lsq_done"), 1)
            act.wait_ge(sem("pe_used"), N2 + 12)
            a(gr[:], ps[:, QQ:QQ + 4, :], ACT.Silu).then_inc(sem("gr_done"), 1)
            act.wait_ge(sem("lsum_ps"), 1)
            a(aA[:, 0, :], ps[:, 3, :], ACT.Sqrt, scale=1.0 / LW, bias=eps).then_inc(sem("lrms_done"), 1)
            make_hi(act, N2 + 13)
            for h in range(RH):
                act.wait_ge(sem("av_ps"), h + 1)
                a(qr[:, h, :], ps[:, (3, 7)[h % 2], :], ACT.Copy).then_inc(sem("o_done"), 1)
                if h == 1:
                    round_mixed(range(4))
            for h in range(RH):
                act.wait_ge(sem("cen_done"), h + 1)
                a(kr[:, h, :], qr[:, h, :], ACT.Square).then_inc(sem("csq_done"), 1)
            for h in range(RH):
                act.wait_ge(sem("hvar_ps"), h + 1)
                a(kr[:, h, :], ps[:, BM[h], :], ACT.Sqrt, scale=1.0 / HD, bias=eps).then_inc(sem("hstd_done"), 1)
            round_mixed(range(4, KD))
            make_hi(act, N2 + 14)
            make_hi(act, N2 + 15)
            make_hi(act, NFFN)
            act.wait_ge(sem("x3_done"), KD)
            make_hi(act, NFFN + 1)
            norm_squares(act, 4, xt)
            norm_root(act, 4, PP)
            norm_round(act, 4, h3)

            def part(n, i, j, down=True):
                p = j[0] % 2
                make_hi(act, n + 2, i)
                act.wait_ge(sem("par_done"), lin(j, i, 1, 1))
                for b in range(2):
                    act.wait_ge(sem("pe_used"), num(n, i, 1, 2 + 2 * b))
                    if b == 0 and down:
                        act.wait_ge(sem("act_lo"), lin(j, i, 1, 0))
                    for m in range(4):
                        last = a((ca, cv)[b][:, m, :], ps[:, (PP, QQ)[b] + m, :], ACT.Identity,
                                 scale=fp[:, p, b, m, 2:3], bias=fp[:, p, b, m, 3:4])
                    last.then_inc(sem("ftap_done"), 1)
                    make_hi(act, n + 3 + 2 * b, i)
                    if b == 0:
                        make_hi(act, n + 4, i)
                act.wait_ge(sem("fa_done"), lin(j, i, 1, 1))
                a(ca[:], ca[:], ACT.Gelu_apprx_tanh).then_inc(sem("gelu_done"), 1)
                if down:
                    make_hi(act, n + 6, i)
                act.wait_ge(sem("prod_done"), lin(j, i, 1, 1))
                a(aH[p][:], ca[:], ACT.Copy).then_inc(sem("act_hi"), 1)
                if down:
                    make_hi(act, n + 7, i)

            part(NFFN, None, (0, 0), down=False)
            with act.Fori(0, NJ // 2 - 1) as i:
                for u in range(2):
                    part(NFFN + 4 + 6 * u, (i, 12), (1 + u, 2))
            part(NFFN + 28, None, (NJ - 1, 0))
            act.wait_ge(sem("dn_taken"), 2 * NJ + 2)
            norm_squares(act, 5, xt)
            norm_root(act, 5, PP)

        def mixed(m):
            return iA[:, m, :] if m < 4 else qr[:, m - 4, :]

        def second_dve(dve, L):
            tt, ts, stt = dve.tensor_tensor, dve.tensor_scalar, dve.scalar_tensor_tensor
            dve.wait_ge(sem("sc_taken"), SCS)
            dve.memset(bd[:], 0.0).then_inc(sem("bd_zero"), 1)
            norm_scale(dve, chains["dve"], 2, xt)
            norm_scale(dve, chains["dve"], 3, xt, h3)
            norm_rest(dve, 3, h3)
            lam = prm[:, P_LAM:P_LAM + 4]
            ts(lz(6), lam, -1.0, 0.0, ALU.mult, ALU.max)
            stt(lz(0), lam, -1.0, lam, ALU.mult, ALU.max).then_inc(sem("laz_done"), 1)
            dve.wait_ge(sem("lze_done"), 1)
            ts(lz(2), lz(1), 1.0, None, ALU.add).then_inc(sem("lzu_done"), 1)
            dve.wait_ge(sem("lzu_done"), 1)
            L(ts(lz(7), lz(2), 1.0, None, ALU.subtract))
            L(ts(lz(8), lz(7), 0.0, None, ALU.is_equal))
            dve.wait_ge(sem("lzl_done"), 1)
            tt(lz(7), lz(7), lz(8), ALU.add)
            L(tt(lz(9), lz(3), lz(8), ALU.add))
            L(dve.reciprocal(lz(7), lz(7)))
            L(tt(lz(9), lz(9), lz(1), ALU.mult))
            L(tt(lz(9), lz(9), lz(7), ALU.mult))
            L(tt(lz(9), lz(9), lz(6), ALU.add))
            ts(lz(4), lz(9), 8.0, None, ALU.mult)
            ts(lz(5), lz(9), -8.0, None, ALU.mult).then_inc(sem("lam_done"), 1)
            dve.wait_ge(sem("tap_done"), 1)
            for tap in range(1, 4):
                for m in range(4):
                    c = P_LCV + 5 * m + 3 - tap
                    last = stt(xc[:, m, tap:], ps[:, PP + m, 0:SEQ - tap], prm[:, c:c + 1], xc[:, m, tap:],
                               ALU.mult, ALU.add)
                if tap < 3:
                    L(last)
            last.then_inc(sem("xc_done"), 1)
            make_lo(dve, N2 + 4)

            def rotate(k, bank, dst):
                cos, sin = (rot[:, r, :].unsqueeze(1).to_broadcast([P, 4, SEQ]) for r in range(2))
                dve.wait_ge(sem("swap_done"), 2 * k + 2)
                tt(dst[:], ps[:, bank:bank + 4, :], cos, ALU.mult).then_inc(sem("cos_done"), 1)
                L(tt(qs[:], qs[:], sin, ALU.mult))
                dve.wait_ge(sem("cos_done"), k + 1)
                tt(dst[:], dst[:], qs[:], ALU.add).then_inc(sem("rot_done"), 1)

            dve.wait_ge(sem("tab_in"), 32)
            dve.wait_ge(sem("pe_used"), N2 + 4)
            rotate(0, QQ, qr)
            make_lo(dve, N2 + 5)
            make_lo(dve, N2 + 6)
            dve.wait_ge(sem("lgate_done"), 8)
            dve.wait_ge(sem("xc_done"), 1)
            L(tt(iA[:], iA[:], xc[:], ALU.mult))
            dve.wait_ge(sem("la_done"), 1)
            dve.wait_ge(sem("lg2_ps"), 8)
            L(tt(xc[:], aA[:], aA[:], ALU.mult))
            dve.wait_ge(sem("tanh_done"), 1)
            stt(rA[:], xc[:], 1.0, rA[:], ALU.add, ALU.mult).then_inc(sem("rad_done"), 1)
            dve.wait_ge(sem("pe_used"), N2 + 6)
            rotate(1, PP, kr)
            make_lo(dve, N2 + 7)
            make_lo(dve, N2 + 8)
            dve.wait_ge(sem("root_done"), 1)
            L(tt(iA[:], iA[:], rA[:], ALU.mult))
            for m in range(4):
                last = dve.tensor_tensor_scan(rA[:, m, :], aA[:, m, :], iA[:, m, :], 0.0, ALU.mult, ALU.add)
            L(last)
            make_lo(dve, N2 + 9)
            make_lo(dve, N2 + 10)
            dve.wait_ge(sem("gl_done"), 1)
            tt(rA[:], rA[:], gl[:], ALU.mult).then_inc(sem("hy_done"), 1)
            for n in range(11, 14):
                make_lo(dve, N2 + n)

            def decay(h):
                dve.wait_ge(sem("sco_ps"), h + 1)
                if h >= 2:
                    dve.wait_ge(sem("av_ps"), h - 1)
                for J in range(4):
                    last = tt(weights(h, J), score(h, J), dec[:, h, 0:SEQ - J * P], ALU.mult)
                last.then_inc(sem("dec_done"), 1)

            def rest_mixed(tiles):
                for m in tiles:
                    dve.wait_ge(sem("mix_hi"), m + 1)
                    tt(xl[:, m, :], mixed(m), xh[:, m, :].bitcast(F32), ALU.subtract).then_inc(sem("mix_lo"), 1)

            decay(0)
            decay(1)
            dve.wait_ge(sem("lrms_done"), 1)
            L(dve.reciprocal(aA[:, 0, :], aA[:, 0, :]))
            for m in range(4):
                stt(iA[:, m, :], rA[:, m, :], prm[:, P_LG + m:P_LG + m + 1], aA[:, 0, :], ALU.mult, ALU.mult) \
                    .then_inc(sem("mix_done"), 1)
            decay(2)
            decay(3)
            rest_mixed(range(4))
            for h in range(RH):
                dve.wait_ge(sem("mean_ps"), h + 1)
                stt(qr[:, h, :], ps[:, BM[h], :], -1.0 / HD, qr[:, h, :], ALU.mult, ALU.add).then_inc(sem("cen_done"), 1)
            dve.wait_ge(sem("cen_done"), RH)
            dve.wait_ge(sem("gr_done"), 1)
            for h in range(RH):
                dve.wait_ge(sem("hstd_done"), h + 1)
                L(dve.reciprocal(kr[:, h, :], kr[:, h, :]))
                L(stt(qr[:, h, :], qr[:, h, :], prm[:, P_RG + h:P_RG + h + 1], kr[:, h, :], ALU.mult, ALU.mult))
                tt(qr[:, h, :], qr[:, h, :], gr[:, h, :], ALU.mult).then_inc(sem("mix_done"), 1)
                if h:
                    rest_mixed([3 + h])
            rest_mixed([KD - 1])
            make_lo(dve, N2 + 14)
            make_lo(dve, N2 + 15)

            def add(bank, half, name, every):
                for m in range(4):
                    last = tt(xt[:, 4 * half + m, :], xt[:, 4 * half + m, :], ps[:, bank + m, :], ALU.add)
                    if every:
                        last.then_inc(sem(name), 1)
                if not every:
                    last.then_inc(sem(name), 1)

            dve.wait_ge(sem("pe_used"), N2 + 14)
            add(QQ, 0, "x3_done", True)
            make_lo(dve, NFFN)
            dve.wait_ge(sem("pe_used"), N2 + 16)
            add(PP, 1, "x3_done", True)
            make_lo(dve, NFFN + 1)
            norm_scale(dve, chains["dve"], 4, xt, h3)
            norm_rest(dve, 4, h3)
            for h in range(2):
                dve.sem_inc(sem("dn_taken"), 1)

            def part(n, i, j, down=True):
                p = j[0] % 2
                dve.tensor_copy(fp[:, p].rearrange("p a b c -> p (a b c)"), prm[:, bass.ds(lin(j, i, 32, P_FF), 32)]) \
                    .then_inc(sem("par_done"), 1)
                dve.wait_ge(sem("par_done"), lin(j, i, 1, 1))
                make_lo(dve, n + 2, i)
                for b in range(2):
                    dst = (ca, cv)[b]
                    dve.wait_ge(sem("ftap_done"), lin(j, i, 2, b + 1))
                    for tap in range(1, 3):
                        if tap == 2:
                            dve.wait_ge(sem("ftap_one"), lin(j, i, 2, b + 1))
                        for m in range(4):
                            last = stt(dst[:, m, tap:], ps[:, (PP, QQ)[b] + m, 0:SEQ - tap], fp[:, p, b, m, 2 - tap:3 - tap],
                                       dst[:, m, tap:], ALU.mult, ALU.add)
                        if tap == 1:
                            last.then_inc(sem("ftap_one"), 1)
                    last.then_inc(sem(("fa_done", "fv_done")[b]), 1)
                    make_lo(dve, n + 3 + 2 * b, i)
                    if b == 0:
                        make_lo(dve, n + 4, i)
                dve.wait_ge(sem("gelu_done"), lin(j, i, 1, 1))
                dve.wait_ge(sem("fv_done"), lin(j, i, 1, 1))
                tt(ca[:], ca[:], cv[:], ALU.mult).then_inc(sem("prod_done"), 1)
                if down:
                    make_lo(dve, n + 6, i)
                    dve.wait_ge(sem("pe_used"), num(n, i, 1, 5))
                    dve.wait_ge(sem("dn_taken"), lin(j, i, 2, 0))
                    add(PP, 0, "dn_taken", False)
                dve.wait_ge(sem("act_hi"), lin(j, i, 1, 1))
                tt(aL[p][:], ca[:], aH[p][:].bitcast(F32), ALU.subtract).then_inc(sem("act_lo"), 1)
                if down:
                    make_lo(dve, n + 7, i)
                    dve.wait_ge(sem("pe_used"), num(n, i, 1, 6))
                    add(QQ, 1, "dn_taken", False)

            part(NFFN, None, (0, 0), down=False)
            with dve.Fori(0, NJ // 2 - 1) as i:
                for u in range(2):
                    part(NFFN + 4 + 6 * u, (i, 12), (1 + u, 2))
            part(NFFN + 28, None, (NJ - 1, 0))
            for half in range(2):
                dve.wait_ge(sem("pe_used"), NFFN + 35 + half)
                dve.wait_ge(sem("dn_taken"), 2 * NJ)
                add((PP, QQ)[half], half, "dn_taken", False)
            dve.wait_ge(sem("dn_taken"), 2 * NJ + 2)
            norm_scale(dve, chains["dve"], 5, xt, h3)

        def second_loads(sp):
            d = sp.dma_start
            sp.wait_ge(sem("sc_taken"), SCS)
            d(rot[:], w["rotary"]).then_inc(sem("tab_in"), 16)
            d(dec[:], w["decay"]).then_inc(sem("tab_in"), 16)
            sp.wait_ge(sem("bd_zero"), 1)
            for r, name in enumerate(("lru_gate_a_w_2", "lru_gate_x_w_2")):
                for odd in range(2):
                    o = 64 * odd
                    d(bd[o:o + 64, r, :, o:o + 64], w[name][odd::2].rearrange("m i j -> i m j")) \
                        .then_inc(sem("bd_in"), 16)
            for n in range(N2 + 4, NFFN):
                load_chunk(sp, n)

            def part(n, i, j, down=True):
                for b in range(2):
                    for h in range(2):
                        load_chunk(sp, n + 2 * b + h, i, ffn_up_chunk(w, lin(j, i, 512, FF2 * b), h))
                if down:
                    for h in range(2):
                        load_chunk(sp, n + 4 + h, i, ffn_down_chunk(w, lin(j, i, 512, -512), h))

            part(NFFN, None, (0, 0), down=False)
            with sp.Fori(0, NJ // 2 - 1) as i:
                for u in range(2):
                    part(NFFN + 4 + 6 * u, (i, 12), (1 + u, 2))
            part(NFFN + 28, None, (NJ - 1, 0))
            for h in range(2):
                load_chunk(sp, NFFN + 34 + h, None, ffn_down_chunk(w, 512 * (NJ - 1), h))
            for k in range(KD):
                sp.wait_ge(sem("nrm_x"), 5 * KD + k + 1)
                d(out[:, k, :], h3[:, k, :]).then_inc(sem("out_done"), 16)
            sp.wait_ge(sem("out_done"), 16 * KD)

        @block.sync
        def _(sp):
            d = sp.dma_start
            d(xin[:], w["x_t"]).then_inc(sem("x_in"), 16)
            d(cst[:], w["consts"][:, 0:NSMALL]).then_inc(sem("cst_in"), 16)
            d(prm[:], w["small"]).then_inc(sem("cst_in"), 16)
            load_chunk(sp, 0)
            d(BS[:].rearrange("p r g h -> p r (g h)"), w["s5b"]).then_inc(sem("s5_in"), 16)
            d(CT[:], w["s5c"]).then_inc(sem("s5_in"), 16)
            for n in range(1, 4):
                load_chunk(sp, n)
            sp.wait_ge(sem("co_done"), 16)
            sp.wait_ge(sem("s5_tables"), 1)
            sp.wait_ge(sem("s_tok"), NT)
            for t in range(NT):
                d(sblk[16 * t:16 * t + 16, :], stok[:, t, :]).then_inc(sem("sblk_in"), 16)
            sp.wait_ge(sem("sblk_in"), 16 * NT)
            sp.wait_ge(sem("hs_ready"), 1)
            for t in range(BL):
                sp.dma_start(INT[t * SH:(t + 1) * SH], HS[:, :, (7 - t) * SH:(7 - t) * SH + P]) \
                    .then_inc(sem("int_in"), 16)
            sp.wait_ge(sem("int_in"), 16 * BL)
            d(wsT[:], w["gmlp_ws_t"]).then_inc(sem("gm_in"), 16)
            d(bsb[:], w["gmlp_bs"]).then_inc(sem("gm_in"), 16)
            for r in range(2):
                d(lnv[:, r, :], w["gmlp_ln"][r].partition_broadcast(P)).then_inc(sem("gm_in"), 16)
            for n in range(4, 11):
                load_chunk(sp, n)
            sp.wait_ge(sem("yblk_done"), 4)
            for t in range(NT):
                d(ytok[:, t, :], yblk[16 * t:16 * t + 16, :]).then_inc(sem("ytok_in"), 16)
            d(wglu[:], w["s5_w_glu"][0].rearrange("(k p) n -> p k n", p=P)).then_inc(sem("glu_in"), 16)
            for n in range(11, NFIRST):
                load_chunk(sp, n)
            sp.wait_ge(sem("ba_done"), 4)
            sp.wait_ge(sem("mrg_b"), 8)
            sp.wait_ge(sem("mg_done"), 8)
            d(xt[:], w["x_t"]).then_inc(sem("x2_in"), 16)
            sp.wait_ge(sem("mh_done"), KD)
            d(wr[:], w["w_router"].rearrange("(k p) e -> p k e", p=P)).then_inc(sem("wr_in"), 16)
            d(cst2[:], w["consts"][:, NSMALL:]).then_inc(sem("wr_in"), 16)
            with sp.Fori(0, NE // 2) as i:
                for u in range(2):
                    for j in range(24):
                        load_chunk(sp, NFIRST + 24 * u + j, (i, 48), expert_chunk(i, u, j))
            for j in range(4):
                load_chunk(sp, NEXP + j)
            second_loads(sp)

        @block.tensor
        def _(pe):
            pe.wait_ge(sem("cst_in"), 32)
            norm_sums(pe, 0, PP)
            pe.wait_ge(sem("xl_done"), KD)
            dense(pe, PP, 0, KD, xh, xl, True, 256)
            dense(pe, QQ, 1, KD, xh, xl, True)
            for q in range(4):
                pe.wait_ge(sem("tab_q"), q + 1)
                if q:
                    pe.wait_ge(sem("vt_done"), 2 * q)
                    pe.wait_ge(sem("hs_done"), 2 * q)
                else:
                    pe.wait_ge(sem("s_tok"), NT)
                for r in range(2):
                    for g in range(GQ):
                        mm = pe.transpose(ps[:, PP + r, g * P:(g + 1) * P],
                                          V[:, r, g].rearrange("p t h -> p (t h)"), ident)
                mm.then_inc(sem("v_ps"), 1)
                for g in range(GQ):
                    o = ps[0:SH, PP + 2 + g // 2, (g % 2) * 256:(g % 2) * 256 + 240]
                    pe.matmul(o, BB[:, 0, GQ * q + g, :], CL[:, 0, g, 1:16, :], start=True, stop=False)
                    mm = pe.matmul(o, BN[:, GQ * q + g, :], CL[:, 1, g, 1:16, :], start=False, stop=True)
                mm.then_inc(sem("h_ps"), 1)
            pe.wait_ge(sem("v_tok"), NT)
            dense(pe, QQ, 3, KD, xh, xl, False)
            pe.wait_ge(sem("vt_done"), 8)
            pe.wait_ge(sem("hs_done"), 8)
            pe.wait_ge(sem("sblkg_done"), 1)
            for g in range(SG):
                mm = pe.transpose(ps[:, PP + 2 + g // 8, (g % 8) * NB:(g % 8 + 1) * NB],
                                  sblkg[:, g * P:(g + 1) * P],
                                  ident[0:NB, 0:NB])
            mm.then_inc(sem("u_ps"), 1)
            pe.wait_ge(sem("u_done"), 2)
            for r in range(2):
                for g in range(SG):
                    mm = pe.matmul(ps[:, PP + 2 * r + g // 8, (g % 8) * NB:(g % 8 + 1) * NB], VT[:, r, g, :],
                                   U[:, g, :], start=True, stop=True)
            mm.then_inc(sem("d_ps"), 1)
            pe.wait_ge(sem("u_tok"), 4)
            dense(pe, QQ, 5, KD, xh, xl, False)
            pe.wait_ge(sem("ds_done"), 8)
            pe.wait_ge(sem("vn_done"), NT)
            pe.wait_ge(sem("gm_in"), 64)
            for half in range(2):
                if half:
                    pe.wait_ge(sem("z_taken"), 4)
                for qq in range(2):
                    q = 2 * half + qq
                    for t in range(NT):
                        mm = pe.matmul(ps[:, PP + 2 * qq + t // 2, (t % 2) * 256:(t % 2 + 1) * 256],
                                       vg[:, t, q * P:(q + 1) * P],
                                       wsT[:, 2 * q:2 * q + 2, :].rearrange("p g t -> p (g t)"),
                                       start=True, stop=True)
                mm.then_inc(sem("z_ps"), 1)
            pe.wait_ge(sem("ga_done"), 4)
            dense(pe, QQ, 7, KD, xh, xl, False)
            pe.wait_ge(sem("z_taken"), 8)
            pe.wait_ge(sem("sn_done"), 4)
            pe.wait_ge(sem("int_in"), 16 * BL)
            for g in range(SG):
                o = ps[0:NB, PP + g // 4, (g % 4) * P:(g % 4 + 1) * P]
                pe.matmul(o, U[:, g, :], INT[:, g, :], start=True, stop=False)
                pe.matmul(o, Sn[:, 0, g, :], CO[:, 0, g, :], start=False, stop=False)
                mm = pe.matmul(o, Sn[:, 1, g, :], CO[:, 1, g, :], start=False, stop=True)
                if g % 4 == 3:
                    mm.then_inc(sem("y_ps"), 1)
            pe.wait_ge(sem("gb_done"), 4)
            dense(pe, QQ, 9, KD, xh, xl, False)
            pe.wait_ge(sem("ytok_in"), 16 * NT)
            pe.wait_ge(sem("yblk_done"), 4)
            for c in range(2):
                for t in range(NT):
                    mm = pe.transpose(ps[:, PP + c, t * P:(t + 1) * P], ytok[:, t, c * P:(c + 1) * P], ident)
            mm.then_inc(sem("yT_ps"), 1)
            pe.wait_ge(sem("yT_done"), 2)
            pe.wait_ge(sem("glu_in"), 16)
            for m in range(2):
                for k in range(2):
                    mm = pe.matmul(ps[:, PP + 2 + m, :], wglu[:, k, m * P:(m + 1) * P], yT[:, k, :],
                                   start=(k == 0), stop=(k == 1))
            mm.then_inc(sem("glu_ps"), 1)
            pe.wait_ge(sem("ga_done"), 8)
            dense(pe, QQ, 11, KD, xh, xl, False)
            pe.wait_ge(sem("ba_done"), 4)
            pe.wait_ge(sem("bb_done"), 2)
            pe.wait_ge(sem("sg_done"), 2)
            for h in range(2):
                if h:
                    pe.wait_ge(sem("mrg_a"), 4 * h)
                dense(pe, PP, 13 + 2 * h, 4, bah, bal, False)
                pe.wait_ge(sem("gb_done"), 8)
                if h:
                    pe.wait_ge(sem("mrg_b"), 4 * h)
                dense(pe, QQ, 14 + 2 * h, 2, bbh, bbl, False)
            pe.wait_ge(sem("mrg_a"), 8)
            pe.wait_ge(sem("mrg_b"), 8)
            pe.wait_ge(sem("mh_done"), KD)
            dense(pe, QQ, 17, KD, xh, xl, False)
            dense(pe, PP, 19, KD, xh, xl, False)
            experts_pe(pe)
            second_pe(pe)

        @block.scalar
        def _(act):
            ch = Chain(act, sem("act_step"))
            a = act.activation
            act.wait_ge(sem("x_in"), 16)
            norm_squares(act, 0, xin)
            norm_root(act, 0, PP)
            norm_round(act, 0, xin)
            for n in range(2):
                make_hi(act, n)
            act.wait_ge(sem("cst_in"), 32)
            a(TY[:, 2, :], prm[:, P_DT:P_DT + SG], ACT.Exp).then_inc(sem("dt_done"), 1)
            act.wait_ge(sem("pe_used"), 1)
            for t in range(NT):
                a(stok[:, t, :], ps[:, PP + t, 0:SW], ACT.Copy).then_inc(sem("s_tok"), 1)
            make_hi(act, 2)
            act.wait_ge(sem("ang_done"), 1)
            a(TY[:, 8, :], TY[:, 3, :], ACT.Exp).then_inc(sem("exp_done"), 1)
            a(TY[:, 9, :], TY[:, 3, :], ACT.Exp, scale=8.0).then_inc(sem("exp_done"), 1)
            a(TY[:, 10, :], TY[:, 6, :], ACT.Sin).then_inc(sem("exp_done"), 1)
            a(TY[:, 11, :], TY[:, 7, :], ACT.Sin).then_inc(sem("exp_done"), 1)
            for q in range(4):
                gs = slice(GQ * q, GQ * q + GQ)
                act.wait_ge(sem("v_ps"), q + 1)
                for r in range(2):
                    a(VT[:, r, gs, :], ps[:, PP + r, :].rearrange("p (g m) -> p g m", g=GQ), ACT.Copy) \
                        .then_inc(sem("vt_done"), 1)
                act.wait_ge(sem("h_ps"), q + 1)
                for j in range(2):
                    a(HS[:, GQ * q + 2 * j:GQ * q + 2 * j + 2, :],
                      ps[0:SH, PP + 2 + j, :].rearrange("p (g m) -> p g m", g=2)[:, :, 0:240], ACT.Copy) \
                        .then_inc(sem("hs_done"), 1)
                for r in range(2):
                    for lo_, i0 in ((0, 9), (64, 0)):
                        a(CO[lo_:lo_ + 64, r, gs, :], CL[lo_:lo_ + 64, r, :, i0:i0 + 8, :].rearrange("p g t h -> p g (t h)"),
                          ACT.Copy, scale=1.0 - 2.0 * r).then_inc(sem("co_done"), 1)
            act.wait_ge(sem("pe_used"), 3)
            act.wait_ge(sem("int_in"), 16 * BL)
            act.wait_ge(sem("s5_tables"), 1)
            for t in range(NT):
                a(vg[:, t, :], ps[:, QQ + t, :], ACT.Gelu).then_inc(sem("v_tok"), 1)
            make_hi(act, 3)
            make_hi(act, 4)
            act.wait_ge(sem("var_done"), 1)
            a(sm[:, 128:132], sm[:, 141:149:2], ACT.Sqrt, bias=eps).then_inc(sem("std_done"), 1)
            act.wait_ge(sem("sblk_in"), 16 * NT)
            a(sblkg[:].rearrange("b (g t h) -> b g t h", g=SG, t=BL),
              sblk[:].rearrange("b (t g h) -> b g t h", t=BL, g=SG), ACT.Copy).then_inc(sem("sblkg_done"), 1)
            act.wait_ge(sem("u_ps"), 1)
            for j in range(2):
                a(U[:, 8 * j:8 * j + 8, :].rearrange("p g b -> p (g b)"), ps[:, PP + 2 + j, :], ACT.Copy) \
                    .then_inc(sem("u_done"), 1)
            act.wait_ge(sem("d_ps"), 1)
            for r in range(2):
                for j in range(2):
                    dps = ps[:, PP + 2 * r + j, :].rearrange("p (g b) -> p g b", b=NB)
                    a(DS[0:64, r, 8 * j:8 * j + 8, :], dps[0:64], ACT.Copy).then_inc(sem("ds_done"), 1)
                    a(DS[64:P, r, 8 * j:8 * j + 8, :], dps[64:P, :, ::-1], ACT.Copy).then_inc(sem("ds_done"), 1)
            act.wait_ge(sem("pe_used"), 5)
            for m in range(4):
                a(uT[:, m, :], ps[:, QQ + m, :], ACT.Gelu).then_inc(sem("u_tok"), 1)
            make_hi(act, 5)
            make_hi(act, 6)

            def gate(dst, n, half, second, name, waits):
                act.wait_ge(sem("pe_used"), n)
                for s, v in waits:
                    act.wait_ge(sem(s), v)
                for m in range(4):
                    c = P_BG + 8 * second + 4 * half + m
                    a(dst[:, m, :], ps[:, QQ + m, :], ACT.Sigmoid, bias=prm[:, c:c + 1]).then_inc(sem(name), 1)

            gate(ga[0], 7, 0, 0, "ga_done", [("z_ps", 2)])
            make_hi(act, 7)
            make_hi(act, 8)
            act.wait_ge(sem("sp_done"), 1)
            for r in range(2):
                a(Sn[0:64, r], DS[0:64, r], ACT.Copy).then_inc(sem("sn_done"), 1)
                a(Sn[64:P, r], DS[64:P, r, :, ::-1], ACT.Copy).then_inc(sem("sn_done"), 1)
            gate(gb[0], 9, 0, 1, "gb_done", [("z_taken", 8), ("vn_done", NT)])
            make_hi(act, 9)
            for j in range(4):
                act.wait_ge(sem("y_ps"), j + 1)
                a(yblk[:].rearrange("b (t g h) -> b g t h", t=BL, g=SG)[:, 4 * j:4 * j + 4],
                  ps[0:NB, PP + j, :].rearrange("b (g t h) -> b g t h", g=4, t=BL), ACT.Gelu) \
                    .then_inc(sem("yblk_done"), 1)
            make_hi(act, 10)
            act.wait_ge(sem("uz_done"), 4)
            for m in range(4):
                a(bah[:, m, :], uT[:, m, :], ACT.Copy).then_inc(sem("bah_done"), 1)
            gate(ga[1], 11, 1, 0, "ga_done", [])
            make_hi(act, 11)
            act.wait_ge(sem("glu_ps"), 1)
            for m in range(2):
                a(sg[:, m, :], ps[:, PP + 2 + m, :], ACT.Sigmoid, bias=prm[:, P_GLU + m:P_GLU + m + 1]).then_inc(sem("sg_done"), 1)
            make_hi(act, 12)
            act.wait_ge(sem("y2_done"), 1)
            for m in range(2):
                a(bbh[:, m, :], sg[:, m, :], ACT.Copy).then_inc(sem("bbh_done"), 1)
            gate(gb[1], 13, 1, 1, "gb_done", [])
            make_hi(act, 13)
            make_hi(act, 14)
            make_hi(act, 15)
            for m in range(4):
                act.wait_ge(sem("mg_done"), m + 1)
                a(xh[:, m, :], ga[0][:, m, :], ACT.Copy).then_inc(sem("mh_hi"), 1)
            make_hi(act, 16)
            make_hi(act, 17)
            for m in range(4):
                act.wait_ge(sem("mg_done"), m + 5)
                a(xh[:, 4 + m, :], ga[1][:, m, :], ACT.Copy).then_inc(sem("mh_hi"), 1)
            for n in range(18, NFIRST):
                make_hi(act, n)
            experts_act(act, a)
            second_act(act, a)

        @block.vector
        def _(dve):
            ch = Chain(dve, sem("dve_step"))
            chains["dve"] = ch
            L = ch.link
            tt, ts, stt = dve.tensor_tensor, dve.tensor_scalar, dve.scalar_tensor_tensor

            def cmul(o, x, y, t, conj=False):
                tt(o[0], x[0], y[0], ALU.mult)
                tt(t[0], x[1], y[1], ALU.mult)
                tt(o[1], x[0], y[1], ALU.mult)
                L(tt(t[1], x[1], y[0], ALU.mult))
                tt(o[0], o[0], t[0], ALU.add if conj else ALU.subtract)
                L(tt(o[1], o[1], t[1], ALU.subtract if conj else ALU.add))

            dve.memset(eps, EPS).then_inc(sem("eps_done"), 1)
            dve.wait_ge(sem("cst_in"), 32)
            norm_scale(dve, ch, 0, xin)
            norm_rest(dve, 0, xin)
            make_lo(dve, 0)
            make_lo(dve, 1)
            y = lambda i: prm[:, P_LRE + SG * i:P_LRE + SG * i + SG] if i < 2 else TY[:, i, :]
            dve.wait_ge(sem("s5_in"), 32)
            dve.wait_ge(sem("dt_done"), 1)
            tt(y(3), y(0), y(2), ALU.mult)
            L(tt(y(4), y(1), y(2), ALU.mult))
            L(ts(y(5), y(4), 1.0 / (2 * math.pi), MAGIC, ALU.mult, ALU.add))
            L(ts(y(5), y(5), MAGIC, None, ALU.subtract))
            L(stt(y(6), y(5), -TWO_PI_HI, y(4), ALU.mult, ALU.add))
            L(stt(y(6), y(5), -TWO_PI_LO, y(6), ALU.mult, ALU.add))
            L(ts(y(6), y(6), 3.1415925, -3.1415925, ALU.min, ALU.max))
            L(stt(y(7), y(6), -1.0, y(6), ALU.mult, ALU.max))
            ts(y(7), y(7), -1.0, HALF_PI, ALU.mult, ALU.add).then_inc(sem("ang_done"), 1)
            make_lo(dve, 2)
            dve.wait_ge(sem("exp_done"), 4)
            tt(y(12), y(8), y(11), ALU.mult)
            tt(y(13), y(8), y(10), ALU.mult)
            tt(y(14), y(0), y(0), ALU.mult)
            L(tt(y(15), y(1), y(1), ALU.mult))
            tt(y(15), y(14), y(15), ALU.add)
            L(ts(y(16), y(12), 1.0, None, ALU.subtract))
            L(dve.reciprocal(y(15), y(15)))
            cmul((y(18), y(19)), (y(0), y(1)), (y(16), y(13)), (y(20), y(21)), conj=True)
            tt(y(18), y(18), y(15), ALU.mult)
            L(tt(y(19), y(19), y(15), ALU.mult))

            def gh(v):
                return v.unsqueeze(2).to_broadcast([P, SG, SH])

            tm = [TMP[:, r, 0:256].rearrange("p (g h) -> p g h", g=SG) for r in range(2)]
            cmul((BB[:, 0], BB[:, 1]), (gh(y(18)), gh(y(19))), (BS[:, 0], BS[:, 1]), tm)
            ts(BN[:], BB[:, 1], -1.0, None, ALU.mult)
            dve.memset(PW[:, 0, :, 0], 1.0)
            dve.memset(PW[:, 1, :, 0], 0.0)
            dve.tensor_copy(PW[:, 0, :, 1], y(12))
            L(dve.tensor_copy(PW[:, 1, :, 1], y(13)))
            for m in (1, 2, 4):
                tm = [TMP[:, r, 0:SG * m].rearrange("p (g k) -> p g k", g=SG) for r in range(2)]
                cmul([PW[:, r, :, m + 1:2 * m + 1] for r in range(2)], [PW[:, r, :, 1:m + 1] for r in range(2)],
                     [PW[:, r, :, m:m + 1].to_broadcast([P, SG, m]) for r in range(2)], tm)
            dve.memset(PT[0:64, :, :, 0:8], 0.0)
            dve.memset(PT[64:P, :, :, 9:17], 0.0)
            dve.tensor_copy(PT[0:64, :, :, 8:17], PW[0:64])
            dve.tensor_copy(PT[64:P, :, :, 0:9], PW[64:P, :, :, 8::-1])
            dve.tensor_copy(PD[0:64], PW[0:64, :, :, 7::-1])
            L(dve.tensor_copy(PD[64:P], PW[64:P, :, :, 0:8]))
            for q in range(4):
                gs = slice(GQ * q, GQ * q + GQ)
                if q:
                    dve.wait_ge(sem("v_ps"), q)
                tm = [TMP[:, r, 0:GQ * P].rearrange("p (g t h) -> p g t h", g=GQ, t=BL) for r in range(2)]
                cmul([V[:, r] for r in range(2)],
                     [PD[:, r, gs].unsqueeze(3).to_broadcast([P, GQ, BL, SH]) for r in range(2)],
                     [BB[:, r, gs].unsqueeze(2).to_broadcast([P, GQ, BL, SH]) for r in range(2)], tm)
                if q:
                    dve.wait_ge(sem("h_ps"), q)
                    dve.wait_ge(sem("co_done"), 4 * q)
                tm = [TMP[:, r].rearrange("p (g t h) -> p g t h", g=GQ, t=17) for r in range(2)]
                ct = CT[:].rearrange("p r (g h) -> p r g h", g=SG)
                cmul([CL[:, r] for r in range(2)],
                     [PT[:, r, gs].unsqueeze(3).to_broadcast([P, GQ, 17, SH]) for r in range(2)],
                     [ct[:, r, gs].unsqueeze(2).to_broadcast([P, GQ, 17, SH]) for r in range(2)], tm)
                dve.sem_inc(sem("tab_q"), 1)
            for s in range(3):
                cmul((y(24 + 2 * s), y(25 + 2 * s)), *[((y(11), y(10)) if s == 0 else (y(22 + 2 * s), y(23 + 2 * s)))] * 2,
                     (y(20), y(21)))
            dve.tensor_copy(WT[:, 0, :, 0], y(28))
            dve.tensor_copy(WT[:, 1, :, 0], y(29))
            dve.memset(RD[:, :, 0:1], 0.0)
            L(dve.tensor_copy(RD[:, :, 1:NB], y(9).unsqueeze(2).to_broadcast([P, SG, NB - 1])))
            for m in (1, 2, 4, 8, 16, 32):
                tm = [TMP[:, r, 0:SG * m].rearrange("p (g k) -> p g k", g=SG) for r in range(2)]
                cmul([WT[:, r, :, m:2 * m] for r in range(2)], [WT[:, r, :, 0:m] for r in range(2)],
                     [WT[:, r, :, m - 1:m].to_broadcast([P, SG, m]) for r in range(2)], tm)
            dve.wait_ge(sem("hs_done"), 8)
            tm = TMP[0:SH, 0, 0:256].rearrange("p (g h) -> p g h", g=SG)
            L(tt(tm, cst[0:SH, C_I16:C_I16 + SH].unsqueeze(1).to_broadcast([SH, SG, SH]),
                 prm[0:SH, P_SD:P_SD + SG].unsqueeze(2).to_broadcast([SH, SG, SH]), ALU.mult))
            tt(HS[:, :, 7 * SH:8 * SH], HS[:, :, 7 * SH:8 * SH], tm, ALU.add).then_inc(sem("hs_ready"), 1)
            dve.wait_ge(sem("hs_ready"), 1)
            dve.sem_inc(sem("s5_tables"), 1)
            make_lo(dve, 3)
            make_lo(dve, 4)
            dve.wait_ge(sem("gm_in"), 64)
            for t in range(NT):
                dve.wait_ge(sem("v_tok"), t + 1)
                L(dve.bn_stats(sm[:, 96 + 6 * t:102 + 6 * t], vg[:, t, :]))
                L(dve.bn_aggr(sm[:, 140 + 2 * t:142 + 2 * t], sm[:, 96 + 6 * t:102 + 6 * t]))
            dve.sem_inc(sem("var_done"), 1)
            dve.wait_ge(sem("std_done"), 1)
            L(dve.reciprocal(sm[:, 132:136], sm[:, 128:132]))
            for t in range(NT):
                L(ts(vg[:, t, :], vg[:, t, :], sm[:, 140 + 2 * t:141 + 2 * t], sm[:, 132 + t:133 + t],
                     ALU.subtract, ALU.mult))
            for t in range(NT):
                last = tt(vg[:, t, :], vg[:, t, :], lnv[:, 0, :], ALU.mult)
            L(last)
            for t in range(NT):
                tt(vg[:, t, :], vg[:, t, :], lnv[:, 1, :], ALU.add).then_inc(sem("vn_done"), 1)
            make_lo(dve, 5)
            dve.wait_ge(sem("ds_done"), 8)
            w2 = [WT[:, r] for r in range(2)]
            E = [Zs[:, r] for r in range(2)]
            cmul(E, w2, [DS[:, r] for r in range(2)], [T2[:, r] for r in range(2)], conj=True)
            flat = lambda v: v.rearrange("p g b -> p (g b)")
            for r in range(2):
                last = dve.tensor_tensor_scan(flat(T2[:, r]), flat(RD[:]), flat(Zs[:, r]), 0.0, ALU.mult, ALU.add)
            L(last)
            make_lo(dve, 6)
            dve.memset(DS[:, :, :, 0:1], 0.0)
            a_, b_ = [w2[r][:, :, 0:NB - 1] for r in range(2)], [T2[:, r, :, 0:NB - 1] for r in range(2)]
            o_ = [DS[:, r, :, 1:NB] for r in range(2)]
            t_ = [Zs[:, r, :, 0:NB - 1] for r in range(2)]
            cmul(o_, a_, b_, t_)
            dve.sem_inc(sem("sp_done"), 1)
            for half in range(2):
                dve.wait_ge(sem("z_ps"), half + 1)
                for qq in range(2):
                    for g2 in range(2):
                        rows = slice(64 * g2, 64 * g2 + 64)
                        z = ps[rows, PP + 2 * qq:PP + 2 * qq + 2, :].rearrange("p a (b c) -> p (a b) c", b=2)
                        z = z[:, :, g2 * P:(g2 + 1) * P]
                        tt(ztmp[rows, qq, :].rearrange("p (t c) -> p t c", t=NT), z,
                           bsb[rows, 2 * half + qq, :].unsqueeze(1).to_broadcast([64, NT, P]), ALU.add) \
                            .then_inc(sem("z_taken"), 1)
                dve.wait_ge(sem("z_taken"), 4 * half + 4)
                dve.wait_ge(sem("u_tok"), 4)
                for qq in range(2):
                    q = 2 * half + qq
                    tt(uT[:, q, :], uT[:, q, :], ztmp[:, qq, :], ALU.mult).then_inc(sem("uz_done"), 1)
                dve.wait_ge(sem("uz_done"), 2 * half + 2)
            for n in range(7, 11):
                make_lo(dve, n)
            for m in range(4):
                dve.wait_ge(sem("bah_done"), m + 1)
                dve.wait_ge(sem("y_ps"), 4)
                tt(bal[:, m, :], uT[:, m, :], bah[:, m, :].bitcast(F32), ALU.subtract).then_inc(sem("ba_done"), 1)
            dve.wait_ge(sem("yT_ps"), 1)
            for c in range(2):
                dve.tensor_copy(yT[:, c, :], ps[:, PP + c, :]).then_inc(sem("yT_done"), 1)
            make_lo(dve, 11)
            dve.wait_ge(sem("sg_done"), 2)
            dve.wait_ge(sem("yT_done"), 2)
            tt(sg[:].rearrange("p a b -> p (a b)"), sg[:].rearrange("p a b -> p (a b)"),
               yT[:].rearrange("p a b -> p (a b)"), ALU.mult).then_inc(sem("y2_done"), 1)
            dve.wait_ge(sem("y2_done"), 1)
            make_lo(dve, 12)
            for m in range(2):
                dve.wait_ge(sem("bbh_done"), m + 1)
                tt(bbl[:, m, :], sg[:, m, :], bbh[:, m, :].bitcast(F32), ALU.subtract).then_inc(sem("bb_done"), 1)
            make_lo(dve, 13)
            make_lo(dve, 14)
            make_lo(dve, 15)
            for h in range(2):
                dve.wait_ge(sem("pe_used"), 14 + 2 * h)
                dve.wait_ge(sem("ga_done"), 4 + 4 * h)
                for m in range(4):
                    tt(ga[h][:, m, :], ga[h][:, m, :], ps[:, PP + m, :], ALU.mult).then_inc(sem("mrg_a"), 1)
                dve.wait_ge(sem("pe_used"), 15 + 2 * h)
                dve.wait_ge(sem("gb_done"), 4 + 4 * h)
                for m in range(4):
                    tt(gb[h][:, m, :], gb[h][:, m, :], ps[:, QQ + m, :], ALU.mult).then_inc(sem("mrg_b"), 1)
                dve.wait_ge(sem("mrg_b"), 4 * h + 4)
                for m in range(4):
                    tt(ga[h][:, m, :], ga[h][:, m, :], gb[h][:, m, :], ALU.add).then_inc(sem("mg_done"), 1)
                if h == 0:
                    make_lo(dve, 16)
                for m in range(4):
                    dve.wait_ge(sem("mh_hi"), 4 * h + m + 1)
                    tt(xl[:, 4 * h + m, :], ga[h][:, m, :], xh[:, 4 * h + m, :].bitcast(F32), ALU.subtract) \
                        .then_inc(sem("mh_done"), 1)
            make_lo(dve, 17)
            make_lo(dve, 18)
            make_lo(dve, 19)
            for h in range(2):
                dve.wait_ge(sem("pe_used"), 19 + 2 * h)
                dve.wait_ge(sem("x2_in"), 16)
                for m in range(4):
                    tt(xt[:, 4 * h + m, :], xt[:, 4 * h + m, :], ps[:, (QQ, PP)[h] + m, :], ALU.add) \
                        .then_inc(sem("x1_done"), 1)
                if h == 0:
                    make_lo(dve, 20)
            experts_dve(dve, L)
            second_dve(dve, L)

    return nc


SLICED = ("w_in", "w_up_a", "w_up_b", "w_out", "w_router", "w_gate", "w_up", "w_down", "w_in_2", "w_out_2",
          "ffn_up_w_2", "ffn_down_w_2", "lru_gate_a_w_2", "lru_gate_x_w_2")


def kernel(**inputs):
    import concourse.bacc as bacc
    from concourse.bass_utils import run_bass_kernel_spmd

    arrays = {name: np.ascontiguousarray(inputs[name]) for name in SLICED + ("s5_w_glu",)}
    arrays |= lay_out({name: np.asarray(a) for name, a in inputs.items()})
    nc = bacc.Bacc("TRN2", target_bir_lowering=False, num_devices=1)
    w = {name: nc.dram_tensor(name, a.shape, mybir.dt.from_np(a.dtype), kind="ExternalInput").ap()
         for name, a in arrays.items()}
    out = nc.dram_tensor("out", (P, KD, SEQ), F32, kind="ExternalOutput").ap()
    build(nc, {name: a[0] if name in SLICED else a for name, a in w.items()}, out)
    r = run_bass_kernel_spmd(nc, [arrays], core_ids=[0])
    return np.ascontiguousarray(r.results[0]["out"].transpose(2, 1, 0)).reshape(1, SEQ, D)
```
